# Optimizing a Trainium2 kernel written in Bass

```python
import jax, jax.numpy as jnp
from jax import lax
import numpy as np

D_MODEL = 1024
BATCH = 1
SEQ = 1024
DEPTH = 2
DEC_BATCH = 1
DEC_SEQ = 256
PAST_LEN = 128

N_MIXERS = 2
N_CONV_LAYERS = (DEPTH + 1) // 2
N_ATTN_LAYERS = DEPTH // 2
CONV_WIDTH = 31
N_HEADS = 16
HEAD_DIM = D_MODEL // N_HEADS
N_KV_HEADS = 4
GROUP = N_HEADS // N_KV_HEADS
WINDOW = 128
BLOCK = 128
D_FF = 2752
FFN_CONV_WIDTH = 3
LN_EPS = 1e-5
NEG_BIG = -1e30
DEEPNORM_ALPHA = (2.0 * DEPTH) ** 0.25
DEEPNORM_BETA = (8.0 * DEPTH) ** -0.25

kernel_name = "hybrid_conformer_swa_convffn_encoder"

def layer_norm(x, g, b):
    xf = x.astype(jnp.float32)
    mu = jnp.mean(xf, -1, keepdims=True)
    var = jnp.mean(jnp.square(xf - mu), -1, keepdims=True)
    y = (xf - mu) * lax.rsqrt(var + LN_EPS)
    return (y * g.astype(jnp.float32) + b.astype(jnp.float32)).astype(x.dtype)

def depthwise_conv(x, w, b):
    pad = w.shape[0] // 2
    y = lax.conv_general_dilated(
        x, w[:, None, :].astype(x.dtype), window_strides=(1,), padding=[(pad, pad)],
        dimension_numbers=('NWC', 'WIO', 'NWC'), feature_group_count=x.shape[-1])
    return y + b

def alibi_slopes():
    return jnp.asarray(2.0 ** (-8.0 * np.arange(1, N_HEADS + 1) / N_HEADS), dtype=jnp.float32)

def conformer_conv(x, w_pw1, b_pw1, w_dw, b_dw, g_n, b_n, w_pw2, b_pw2):
    h = x @ w_pw1 + b_pw1
    a, gate = jnp.split(h, 2, axis=-1)
    h = a * jax.nn.sigmoid(gate)
    h = depthwise_conv(h, w_dw, b_dw)
    h = jax.nn.silu(layer_norm(h, g_n, b_n))
    return h @ w_pw2 + b_pw2

def windowed_gqa(x, w_q, w_kv, w_o, sink):
    B, S, _ = x.shape
    nb = S // BLOCK
    q = (x @ w_q).reshape(B, nb, BLOCK, N_KV_HEADS, GROUP, HEAD_DIM)
    kv = (x @ w_kv).reshape(B, S, 2, N_KV_HEADS, HEAD_DIM)
    k, v = kv[:, :, 0], kv[:, :, 1]

    def bands(t):
        tp = jnp.pad(t, ((0, 0), (BLOCK, BLOCK), (0, 0), (0, 0)))
        tp = tp.reshape(B, nb + 2, BLOCK, N_KV_HEADS, HEAD_DIM)
        return jnp.concatenate([tp[:, :-2], tp[:, 1:-1], tp[:, 2:]], axis=2)

    kb, vb = bands(k), bands(v)
    scores = jnp.einsum('bnqgrd,bnkgd->bngrqk', q, kb,
                        preferred_element_type=jnp.float32) * (HEAD_DIM ** -0.5)
    blk = jnp.arange(nb)[:, None] * BLOCK
    q_pos = blk + jnp.arange(BLOCK)[None, :]
    k_pos = blk - BLOCK + jnp.arange(3 * BLOCK)[None, :]
    dist = jnp.abs(q_pos[:, :, None] - k_pos[:, None, :])
    valid = (dist <= WINDOW) & (k_pos[:, None, :] >= 0) & (k_pos[:, None, :] < S)
    slopes = alibi_slopes().reshape(N_KV_HEADS, GROUP)
    scores = jnp.where(valid[None, :, None, None],
                       scores - slopes[None, None, :, :, None, None]
                       * dist[None, :, None, None].astype(jnp.float32),
                       NEG_BIG)
    sink_l = sink.astype(jnp.float32).reshape(N_KV_HEADS, GROUP)[None, None, :, :, None, None]
    m = jnp.maximum(jnp.max(scores, -1, keepdims=True), sink_l)
    p = jnp.exp(scores - m)
    probs = (p / (jnp.sum(p, -1, keepdims=True) + jnp.exp(sink_l - m))).astype(x.dtype)
    out = jnp.einsum('bngrqk,bnkgd->bnqgrd', probs, vb)
    return out.reshape(B, S, N_HEADS * HEAD_DIM) @ w_o

def conv_ffn(x, w_up, w_dw, b_dw, w_down):
    h = depthwise_conv(x @ w_up, w_dw, b_dw)
    g, u = jnp.split(h, 2, axis=-1)
    return (jax.nn.silu(g) * u) @ w_down

def encoder_trunk(x, conv_w_pw1, conv_b_pw1, conv_w_dw, conv_b_dw, conv_norm_g, conv_norm_b,
                  conv_w_pw2, conv_b_pw2, attn_w_q, attn_w_kv, attn_w_o, attn_sink,
                  ffn_w_up, ffn_w_dw, ffn_b_dw, ffn_w_down,
                  ln_mix_g, ln_mix_b, ln_ffn_g, ln_ffn_b):
    for i in range(DEPTH):
        j = i // N_MIXERS
        if i % N_MIXERS == 0:
            mix = conformer_conv(x, conv_w_pw1[j], conv_b_pw1[j], conv_w_dw[j], conv_b_dw[j],
                                 conv_norm_g[j], conv_norm_b[j], conv_w_pw2[j], conv_b_pw2[j])
        else:
            mix = windowed_gqa(x, attn_w_q[j], attn_w_kv[j], attn_w_o[j], attn_sink[j])
        x = layer_norm(DEEPNORM_ALPHA * x + mix, ln_mix_g[i], ln_mix_b[i])
        f = conv_ffn(x, ffn_w_up[i], ffn_w_dw[i], ffn_b_dw[i], ffn_w_down[i])
        x = layer_norm(DEEPNORM_ALPHA * x + f, ln_ffn_g[i], ln_ffn_b[i])
    return x

def setup_inputs(seed: int = 0) -> dict:
    key = jax.random.key(seed)
    ks = jax.random.split(key, 32)
    D, F, KVD = D_MODEL, D_FF, N_KV_HEADS * HEAD_DIM
    nA, nB = N_CONV_LAYERS, N_ATTN_LAYERS

    def nrm(k, shape, scale):
        return jax.random.normal(k, shape, jnp.float32) * scale

    def gain(k, shape):
        return 1.0 + nrm(k, shape, 0.02)

    beta = DEEPNORM_BETA
    w_k = nrm(ks[10], (nB, D, KVD), D ** -0.5)
    w_v = nrm(ks[11], (nB, D, KVD), D ** -0.5 * beta)
    return {
        "x_prompt": nrm(ks[0], (BATCH, SEQ, D), 1.0),
        "x_sample": nrm(ks[1], (DEC_BATCH, DEC_SEQ, D), 1.0),
        "conv_w_pw1": nrm(ks[2], (nA, D, 2 * D), D ** -0.5),
        "conv_b_pw1": nrm(ks[3], (nA, 2 * D), 0.02),
        "conv_w_dw": nrm(ks[4], (nA, CONV_WIDTH, D), CONV_WIDTH ** -0.5),
        "conv_b_dw": nrm(ks[5], (nA, D), 0.02),
        "conv_norm_g": gain(ks[6], (nA, D)),
        "conv_norm_b": nrm(ks[7], (nA, D), 0.02),
        "conv_w_pw2": nrm(ks[8], (nA, D, D), D ** -0.5 * beta),
        "conv_b_pw2": nrm(ks[9], (nA, D), 0.02),
        "attn_w_q": nrm(ks[12], (nB, D, N_HEADS * HEAD_DIM), D ** -0.5),
        "attn_w_kv": jnp.concatenate([w_k, w_v], axis=-1),
        "attn_w_o": nrm(ks[13], (nB, N_HEADS * HEAD_DIM, D), D ** -0.5 * beta),
        "attn_sink": nrm(ks[14], (nB, N_HEADS), 0.5),
        "ffn_w_up": nrm(ks[15], (DEPTH, D, 2 * F), D ** -0.5),
        "ffn_w_dw": nrm(ks[16], (DEPTH, FFN_CONV_WIDTH, 2 * F), FFN_CONV_WIDTH ** -0.5),
        "ffn_b_dw": nrm(ks[17], (DEPTH, 2 * F), 0.02),
        "ffn_w_down": nrm(ks[18], (DEPTH, F, D), F ** -0.5 * beta),
        "ln_mix_g": gain(ks[19], (DEPTH, D)),
        "ln_mix_b": nrm(ks[20], (DEPTH, D), 0.02),
        "ln_ffn_g": gain(ks[21], (DEPTH, D)),
        "ln_ffn_b": nrm(ks[22], (DEPTH, D), 0.02),
    }

def reference(x_prompt, x_sample, conv_w_pw1, conv_b_pw1, conv_w_dw, conv_b_dw, conv_norm_g,
              conv_norm_b, conv_w_pw2, conv_b_pw2, attn_w_q, attn_w_kv, attn_w_o, attn_sink,
              ffn_w_up, ffn_w_dw, ffn_b_dw, ffn_w_down, ln_mix_g, ln_mix_b, ln_ffn_g, ln_ffn_b):
    y_prompt = encoder_trunk(x_prompt, conv_w_pw1, conv_b_pw1, conv_w_dw, conv_b_dw, conv_norm_g,
                             conv_norm_b, conv_w_pw2, conv_b_pw2, attn_w_q, attn_w_kv, attn_w_o,
                             attn_sink, ffn_w_up, ffn_w_dw, ffn_b_dw, ffn_w_down,
                             ln_mix_g, ln_mix_b, ln_ffn_g, ln_ffn_b)
    y_sample = encoder_trunk(x_sample, conv_w_pw1, conv_b_pw1, conv_w_dw, conv_b_dw, conv_norm_g,
                             conv_norm_b, conv_w_pw2, conv_b_pw2, attn_w_q, attn_w_kv, attn_w_o,
                             attn_sink, ffn_w_up, ffn_w_dw, ffn_b_dw, ffn_w_down,
                             ln_mix_g, ln_mix_b, ln_ffn_g, ln_ffn_b)
    return (y_prompt, y_sample)


_drawn_inputs = setup_inputs


def setup_inputs(seed=0):
    import zlib

    import numpy as np

    out = dict(_drawn_inputs(seed))
    spreads = {}
    factors = {'conv_b_pw1': 8.0,
     'conv_b_dw': 6.591,
     'conv_norm_g': 22.647,
     'conv_norm_b': 24.206,
     'conv_b_pw2': 21.607,
     'attn_sink': 8.0,
     'ffn_b_dw': 6.666}
    for name, (base, spread) in spreads.items():
        noise = np.random.default_rng([zlib.crc32(name.encode()), seed]).standard_normal(out[name].shape)
        drawn = base * np.exp(spread * noise) if base else spread * noise
        out[name] = __import__('jax').numpy.asarray(drawn.astype(out[name].dtype))
    for name, factor in factors.items():
        out[name] = (out[name] * factor).astype(out[name].dtype)
    return out
```

```python
from contextlib import ExitStack

import concourse.bass as bass
from concourse import mybir

F32 = mybir.dt.float32
F32R = mybir.dt.float32r
I32 = mybir.dt.int32
ALU = mybir.AluOpType
ACT = mybir.ActivationFunctionType
AX_X = mybir.AxisListType.X

P = 128
HALF = 512
RAW = 4
RING = 8


class Count:

    def __init__(self):
        self.n = 0
        self.loop = 0
        self.start = 0

    def one(self):
        self.n += 1
        return 1

    def now(self):
        return self.loop + self.n

    def rounds(self, engine, count, body):
        before = self.n
        body(0, True)
        per_round = self.n - before
        with engine.Fori(1, count) as i:
            self.loop = i * per_round - per_round
            body(i, False)
        assert self.n == before + 2 * per_round
        self.n, self.loop = before + count * per_round, 0


def trunk(nc, w, out_prompt, out_sample, residual_dram):
    D = w["x_prompt"].shape[2]
    S0, S1 = w["x_prompt"].shape[1], w["x_sample"].shape[1]
    T = S0 + S1
    TT = T // P
    KT = D // P
    T0 = S0 // P
    TAPS = w["conv_w_dw"].shape[1]
    PAD = TAPS // 2
    NKV = 4
    NH = w["attn_sink"].shape[1]
    GROUP = NH // NKV
    HD = D // NH
    KVD = NKV * HD
    F = w["ffn_w_down"].shape[1]
    FT = F // P
    FR = F - FT * P
    DEPTH = w["ffn_w_up"].shape[0]
    ALPHA = (2.0 * DEPTH) ** 0.25
    EPS = 1e-5
    SLOPES = [2.0 ** (-8.0 * (h + 1) / NH) for h in range(NH)]
    FAR = 1.0e35
    CHUNKS = [(0, HALF), (HALF, HALF), (S0, S1)]
    assert S0 == 2 * HALF and S1 <= HALF and FR == 64 and D == 2 * HALF and HD == 64
    GROUPS = (FT - 1) // 2
    assert 2 * GROUPS + 1 == FT and GROUPS % 2 == 0
    CONV_COLS = 2 * FT + 1

    UNIT = 2
    B_PW1 = 0
    B_PW2 = B_PW1 + 2 * KT * UNIT
    B_FFN0 = B_PW2 + 2 * KT
    N_FFN = GROUPS * 12 + 10
    B_KV = B_FFN0 + N_FFN
    B_Q = B_KV + 8
    B_O = B_Q + KT * UNIT
    B_FFN1 = B_O + 2 * KT
    N_PIECES = B_FFN1 + N_FFN
    FFN_BASE = [B_FFN0, B_FFN1]

    with ExitStack() as ctx:
        def sb(name, shape, dt=F32, where=ctx):
            return where.enter_context(nc.sbuf_tensor(name, shape, dt))

        def sem(name):
            return ctx.enter_context(nc.semaphore(name))

        XH = sb("x_hi", [P, KT, T], F32R)
        XL = sb("x_lo", [P, KT, T], F32R)
        y = sb("y", [P, TT, D])
        raw = sb("raw_pieces", [P, RAW, HALF])
        WH = sb("w_hi", [P, RING, HALF], F32R)
        WL = sb("w_lo", [P, RING, HALF], F32R)
        ident = sb("ident", [P, P])
        ffn_tab = sb("ffn_conv_table", [P, DEPTH, 4, CONV_COLS])
        conv_tab = sb("conv_table", [P, KT, TAPS])
        chan = sb("channel_table", [P, 5, KT])
        stats = sb("stats", [P, 2, 2, 6])
        mv = sb("mean_var", [P, TT, 2])
        std = sb("std", [P, TT])
        rstd = sb("rstd", [P, TT])
        eps = sb("eps", [P, 1])
        dist = sb("distance", [P, 3 * P])
        sink = sb("sink_rows", [P, NH])
        with ExitStack() as a:
            glu = sb("glu", [P, PAD + S0 + PAD + S1 + PAD], where=a)
            acc = sb("conv_acc", [P, S0 + PAD + S1], where=a)
            sig = sb("sigmoid", [P, HALF], where=a)
            normed = sb("conv_normed", [P, 2, D], where=a)
            act_out = sb("conv_silu", [P, 2, KT, P], where=a)
        with ExitStack() as a:
            ffn_rows = sb("ffn_rows", [CONV_COLS, DEPTH, 4, P], where=a)
            conv_rows = sb("conv_rows", [TAPS, D], where=a)
            chan_rows = sb("chan_rows", [5 * KT, P], where=a)
            dist_i = sb("distance_int", [P, 3 * P], I32, where=a)
        with ExitStack() as a:
            gain = sb("gain_rows", [P, D], where=a)
            shift = sb("shift_rows", [P, D], where=a)
            HH = sb("h_hi", [P, 2, T], F32R, where=a)
            HL = sb("h_lo", [P, 2, T], F32R, where=a)
            gu_raw = sb("gate_up_raw", [P, 2, 1 + S0 + 1 + S1 + 1], where=a)
            g_conv = sb("gate_conv", [P, HALF + 1], where=a)
            u_conv = sb("up_conv", [P, HALF + 1], where=a)
        with ExitStack() as a:
            sb("gain_below", [P, D], where=a)
            sb("shift_below", [P, D], where=a)
            pw2_bias = sb("pw2_bias_rows", [P, D], where=a)
        with ExitStack() as a:
            k_sb = sb("k", [P, NKV // 2, T], where=a)
            v_sb = sb("v", [P, TT, KVD], where=a)
            probs = sb("probs", [P, 3, GROUP, 3 * P], where=a)
            probsT = sb("probs_T", [P, 2, GROUP * P], where=a)
            nmax = sb("minus_max", [P, 3, GROUP], where=a)
            sexp = sb("sink_exp", [P, 3, GROUP], where=a)
            ssum = sb("exp_sum", [P, 3, GROUP], where=a)
            srec = sb("one_over_denominator", [P, 3, GROUP], where=a)
        conv = y[:].rearrange("p t d -> p (t d)").rearrange("p (k t) -> p k t", k=KT)
        q_sb = conv

        bank = [ctx.enter_context(nc.psum_tensor(f"bank{i}", [P, HALF], F32)) for i in range(8)]

        raw_landed = [sem(f"raw_landed{i}") for i in range(RAW)]
        piece_hi = sem("piece_hi")
        piece_split = sem("piece_split")
        piece_used = sem("piece_used")
        x_landed = [sem(f"x_landed{i}") for i in range(TT)]
        tables_landed = sem("tables_landed")
        consts_ready = sem("consts_ready")
        pool_step = sem("pool_step")
        pool_passed = sem("pool_passed")
        tab_turned = sem("tables_turned")
        tab_kept = sem("tables_kept")
        vec_step = sem("vec_step")
        act_passed = sem("act_passed")
        turned = sem("tile_turned")
        turned_hi = sem("turned_hi")
        turned_lo = sem("turned_lo")
        pw1_done = sem("pw1_done")
        sig_ready = sem("sig_ready")
        glu_done = sem("glu_done")
        conv_done = sem("conv_done")
        ct_turned = sem("conv_tile_turned")
        ct_read = sem("conv_tile_read")
        cn_ready = sem("conv_normed_ready")
        cn_turned = sem("conv_normed_turned")
        silu_ready = sem("silu_ready")
        silu_hi = sem("silu_hi")
        silu_lo = sem("silu_lo")
        std_ready = sem("std_ready")
        conv_var = sem("conv_variances_ready")
        conv_std = sem("conv_deviations_ready")
        var_ready = sem("var_ready")
        gains_landed = sem("gains_landed")
        ln_ready = sem("ln_ready")
        scaled = sem("residual_scaled")
        out_stored = sem("out_stored")
        res_stored = sem("residual_stored")
        res_landed = [sem(f"res_landed{i}") for i in range(TT)]
        proj_done = sem("proj_done")
        proj_kept = sem("proj_kept")
        ffn_up = sem("ffn_up_done")
        ffn_raw = sem("ffn_raw_kept")
        ffn_conv = sem("ffn_conv_done")
        ffn_gc = sem("ffn_gate_ready")
        ffn_silu = sem("ffn_silu_ready")
        ffn_h = sem("ffn_h_ready")
        down_done = sem("ffn_down_done")
        down_kept = sem("ffn_down_kept")
        qkv_done = sem("qkv_done")
        qkv_kept = sem("qkv_kept")
        score_done = sem("score_done")
        score_kept = sem("score_kept")
        max_ready = sem("max_ready")
        exp_ready = sem("exp_ready")
        recip_ready = sem("recip_ready")
        probs_ready = sem("probs_ready")
        probs_ready_pool = sem("probs_ready_pool")
        probs_turned = sem("probs_turned")
        probs_T_kept = sem("probs_T_kept")
        av_done = sem("av_done")
        av_hi = sem("av_hi")
        av_lo = sem("av_lo")

        block = ctx.enter_context(nc.Block())

        x_rows = [w["x_prompt"][0, t * P:(t + 1) * P, :] for t in range(T0)] + \
                 [w["x_sample"][0, t * P:(t + 1) * P, :] for t in range(TT - T0)]
        out_rows = [out_prompt[0, t * P:(t + 1) * P, :] for t in range(T0)] + \
                   [out_sample[0, t * P:(t + 1) * P, :] for t in range(TT - T0)]
        residual_rows = [residual_dram[t * P:(t + 1) * P, :] for t in range(TT)]

        def cols(t):
            return slice(t * P, (t + 1) * P)

        transfers = [1] * N_PIECES
        for p in [*range(B_Q, B_FFN1), *(b + 12 * GROUPS + 4 + h for b in FFN_BASE for h in range(2))]:
            transfers[p] = 2

        def landed(p):
            return 16 * sum(transfers[p % RAW:p + 1:RAW])

        @block.sync
        def _(sp):
            def slot_free(p, earlier=0):
                if p >= RAW:
                    sp.wait_ge(piece_split, earlier + p - RAW + 1)

            def column_piece(p, mat, col, half, n=4, width=P, earlier=0):
                view = mat.rearrange("(k p) f -> p k f", p=P)
                slot_free(p, earlier)
                sp.dma_start(raw[:, p % RAW, :].rearrange("p (k f) -> p k f", f=width),
                             view[:, n * half:n * (half + 1), bass.ds(col, width)]
                             ).then_inc(raw_landed[p % RAW], 16)

            def paired_piece(p, view, half):
                slot_free(p)
                for s in range(2):
                    dst = raw[:, p % RAW, :].rearrange("p (k s f) -> p k s f", k=4, s=2)
                    sp.dma_start(dst[:, :, s, :], view[:, 4 * half:4 * half + 4, s, :]
                                 ).then_inc(raw_landed[p % RAW], 16)

            def row_piece(p, rows, earlier=0, height=P):
                slot_free(p, earlier)
                sp.dma_start(raw[0:height, p % RAW, :], rows).then_inc(raw_landed[p % RAW], 16)

            for p in range(8):
                column_piece(B_PW1 + p, w["conv_w_pw1"][0], (p // 2 % 2) * D + (p // 4) * P, p % 2)
            with sp.Fori(1, KT // 2) as i:
                for p in range(8):
                    c, j = p // 4, p % 4
                    sp.wait_ge(piece_split, i * 8 + p - RAW + 1)
                    view = w["conv_w_pw1"][0].rearrange("(k p) f -> p k f", p=P)
                    sp.dma_start(raw[:, p % RAW, :].rearrange("p (k f) -> p k f", f=P),
                                 view[:, 4 * (j % 2):4 * (j % 2) + 4,
                                      bass.ds(i * 2 * P + (j // 2) * D + c * P, P)]
                                 ).then_inc(raw_landed[p % RAW], 16)
            for n in range(2):
                for k in range(KT):
                    row_piece(B_PW2 + n * KT + k, w["conv_w_pw2"][0, cols(k), n * HALF:(n + 1) * HALF])

            def ffn_pieces(layer):
                up, down, base = w["ffn_w_up"][layer], w["ffn_w_down"][layer], FFN_BASE[layer]
                with sp.Fori(0, GROUPS // 2) as i:
                    for g in range(2):
                        for j in range(8):
                            f = 2 * g + j // 4
                            column_piece(base + 12 * g + j, up, i * 4 * P + f * P + (j // 2 % 2) * F,
                                         j % 2, earlier=i * 24)
                        for j in range(4):
                            row_piece(base + 12 * g + 8 + j,
                                      down[bass.ds(i * 4 * P + (2 * g + j % 2) * P, P),
                                           (j // 2) * HALF:(j // 2 + 1) * HALF], earlier=i * 24)
                p = base + 12 * GROUPS
                for j in range(4):
                    column_piece(p + j, up, (FT - 1) * P + (j // 2) * F, j % 2)
                rest = up.rearrange("(k p) (s f) -> p k s f", p=P, s=2)[:, :, :, FT * P:F]
                for half in range(2):
                    paired_piece(p + 4 + half, rest, half)
                for j in range(4):
                    n = j // 2
                    if j % 2 == 0:
                        row_piece(p + 6 + j, down[(FT - 1) * P:FT * P, n * HALF:(n + 1) * HALF])
                    else:
                        row_piece(p + 6 + j, down[FT * P:F, n * HALF:(n + 1) * HALF], height=FR)

            ffn_pieces(0)
            for j in range(4):
                column_piece(B_KV + j, w["attn_w_kv"][0], (j // 2) * P, j % 2)
            for j in range(4):
                column_piece(B_KV + 4 + j, w["attn_w_kv"][0], KVD, j, n=2, width=KVD)
            q_cols = w["attn_w_q"][0].rearrange("(k p) (rr s r d) -> p k rr s r d", p=P, rr=2, s=2, r=GROUP)
            for c in range(KT):
                for half in range(2):
                    paired_piece(B_Q + 2 * c + half, q_cols[:, :, c // GROUP, :, c % GROUP, :], half)
            o_rows = w["attn_w_o"][0].rearrange("(rr s r d) n -> rr s r d n", rr=2, s=2, r=GROUP)
            for n in range(2):
                for k in range(KT):
                    p = B_O + n * KT + k
                    slot_free(p)
                    for s in range(2):
                        sp.dma_start(raw[s * HD:(s + 1) * HD, p % RAW, :],
                                     o_rows[k // GROUP, s, k % GROUP, :, n * HALF:(n + 1) * HALF]
                                     ).then_inc(raw_landed[p % RAW], 16)
            ffn_pieces(1)

        ATT = [(n, rr, par) for n in range(TT) for rr in range(2) for par in range(2)]

        def key_blocks(n):
            lo, hi = (0, T0) if n < T0 else (T0, TT)
            return range(max(lo, n - 1), min(hi, n + 2))

        KEYS_TO = [sum(len(key_blocks(n)) for n, _, _ in ATT[:i]) for i in range(len(ATT) + 1)]
        SCORE_BANKS = (0, 1, 7)

        N_TABLE_DMAS = 8 * DEPTH + 6
        FT_ALL = FT + 1
        N_DOWN = 20 * (GROUPS + 1)
        N_PROJ = 2 * TT
        GAINS_BY = [48, 80, 112, 144]
        H_CHUNK = [0 if (t + 1) * P < HALF else 1 if t < T0 else 2 for t in range(TT)]
        CONV_CHUNKS = [(0, HALF - 1, 0), (HALF - 1, HALF + 1, HALF - 1), (S0, S1, S0 + 1)]
        RAW_COL = [1, 1 + HALF, 1 + S0 + 1]

        def bank_before(m):
            same = [b for b in range(m) if b % TT % 8 == m % TT % 8]
            return same[-1] if same else None

        BLOCKS = [(0, 4), (4, 8), (8, TT)]

        @block.gpsimd
        def _(pool):
            step = Count()
            pool.memset(ident[:], 0.0).then_inc(pool_step, step.one())
            pool.wait_ge(pool_step, step.now())
            pool.affine_select(out=ident[:], in_=ident[:], compare_op=ALU.not_equal, fill=1.0, base=0,
                               pattern=[[-1, P]], channel_multiplier=1).then_inc(consts_ready, 1)
            pool.memset(eps[:], EPS).then_inc(consts_ready, 1)

            def split(p, landed_value, used_value):
                pool.wait_ge(raw_landed[p % RAW], landed_value)
                if used_value is not None:
                    pool.wait_ge(piece_used, used_value)
                pool.sem_inc(pool_passed, 1)
                pool.tensor_copy(WH[:, p % RING, :], raw[:, p % RAW, :]).then_inc(piece_hi, 1)

            def split_low(p, hi_value):
                pool.wait_ge(piece_hi, hi_value)
                pool.tensor_tensor(WL[:, p % RING, :], raw[:, p % RAW, :], WH[:, p % RING, :].bitcast(F32),
                                   ALU.subtract).then_inc(piece_split, 1)

            pool.iota(dist_i[:], pattern=[[-1, 3 * P]], base=P, channel_multiplier=1).then_inc(pool_step, step.one())
            pool.wait_ge(pool_step, step.now())
            pool.tensor_copy(dist[:], dist_i[:]).then_inc(pool_step, step.one())
            pool.wait_ge(pool_step, step.now())
            pool.affine_select(out=dist[:], in_=dist[:], compare_op=ALU.is_ge, fill=FAR, base=0,
                               pattern=[[1, 3 * P]], channel_multiplier=-1).then_inc(pool_step, step.one())
            pool.wait_ge(pool_step, step.now())
            pool.affine_select(out=dist[:], in_=dist[:], compare_op=ALU.is_ge, fill=FAR, base=2 * P,
                               pattern=[[-1, 3 * P]], channel_multiplier=1).then_inc(consts_ready, 1)

            for p in range(RING):
                split(p, landed(p), None)
                split_low(p, p + 1)
            def stretch(first, end):
                rounds = (end - first) // RING
                per = 16 * (RING // RAW) * transfers[first]
                if rounds > 1:
                    with pool.Fori(0, rounds) as i:
                        for p in range(first, first + RING):
                            split(p, i * per + landed(p), i * RING + p - RING + 1)
                            split_low(p, i * RING + p + 1)
                    first += rounds * RING
                for p in range(first, end):
                    split(p, landed(p), p - RING + 1)
                    split_low(p, p + 1)

            def normalise_half(i):
                nk, b = len(key_blocks(ATT[i][0])) * P, i % 3
                pool.wait_ge(recip_ready, i + 1)
                for r in range(GROUP // 2, GROUP):
                    ins = pool.tensor_scalar(probs[:, b, r, 0:nk], probs[:, b, r, 0:nk], srec[:, b, r:r + 1],
                                             None, ALU.mult)
                ins.then_inc(probs_ready_pool, 1)

            rest0, rest1 = (b + 12 * GROUPS + 4 for b in FFN_BASE)
            stretch(RING, rest0)
            stretch(rest0, rest0 + 2)
            stretch(rest0 + 2, B_Q)
            stretch(B_Q, B_O)
            for i in range(len(ATT)):
                if i < RING - 1:
                    stretch(B_O + i, B_O + i + 1)
                normalise_half(i)
            stretch(B_O + RING - 1, B_FFN1)
            stretch(B_FFN1, rest1)
            stretch(rest1, rest1 + 2)
            stretch(rest1 + 2, N_PIECES)

        @block.tensor
        def _(pe):
            owed = [False]

            def product(out, left, right, first, last, uses=0):
                mm = pe.matmul(out, left[0], right[0], start=first, stop=False)
                if owed[0]:
                    mm.then_inc(piece_used, 1)
                pe.matmul(out, left[0], right[1], start=False, stop=False)
                owed[0] = bool(uses)
                return pe.matmul(out, left[1], right[0], start=False, stop=last)

            def rounds(count, body):
                body(0, True)
                with pe.Fori(1, count) as i:
                    body(i, False)

            def wblock(p, k):
                s = (p + k // 4) % RING
                c = slice((k % 4) * P, (k % 4 + 1) * P)
                return WH[:, s, c], WL[:, s, c]

            def xpart(k, c0, n):
                return XH[:, k, c0:c0 + n], XL[:, k, c0:c0 + n]

            def turn_tile(use, t):
                for half in range(2):
                    b = 2 * TT * use + 2 * t + half
                    if b >= 4:
                        pe.wait_ge(turned_lo, b - 3)
                    for j in range(4):
                        mm = pe.transpose(bank[b % 4][:, cols(j)], y[:, t, cols(4 * half + j)], ident[:])
                    mm.then_inc(turned, 1)

            pe.wait_ge(consts_ready, 2)
            for t in range(TT):
                pe.wait_ge(x_landed[t], 16)
                turn_tile(0, t)
            pe.wait_ge(consts_ready, 3)
            pe.wait_ge(tables_landed, 16 * N_TABLE_DMAS)
            for layer in range(DEPTH):
                for tap in range(4):
                    o = (4 * layer + tap) * CONV_COLS
                    mm = pe.transpose(bank[4][:, o:o + CONV_COLS], ffn_rows[:, layer, tap, :],
                                      ident[0:CONV_COLS, 0:CONV_COLS])
            mm.then_inc(tab_turned, 1)
            for k in range(KT):
                mm = pe.transpose(bank[5][:, k * TAPS:(k + 1) * TAPS], conv_rows[:, cols(k)],
                                  ident[0:TAPS, 0:TAPS])
            mm.then_inc(tab_turned, 1)
            pe.transpose(bank[6][:, 0:5 * KT], chan_rows[:, :], ident[0:5 * KT, 0:5 * KT]).then_inc(tab_turned, 1)

            def back_tile(t):
                pe.wait_ge(cn_ready, t + 1)
                if t >= 2:
                    pe.wait_ge(silu_ready, t - 1)
                for k in range(KT):
                    mm = pe.transpose(bank[4 + 2 * (t % 2) + k // 4][:, cols(k % 4)], normed[:, t % 2, cols(k)],
                                      ident[:])
                mm.then_inc(cn_turned, 1)

            def pair_chunk(p, left, right, c0, n, last_chunk):
                for b, q in ((left, p), (right, p + UNIT)):
                    for k in range(KT):
                        mm = product(bank[b][:, 0:n], wblock(q, k), xpart(k, c0, n),
                                     k == 0, k == KT - 1, uses=last_chunk and k % 4 == 3)
                return mm

            pe.wait_ge(turned_lo, 2 * TT)

            def pw1_round(i, first):
                for c in range(2):
                    pe.wait_ge(piece_split, i * 8 + 4 * c + 4)
                    for ch, (c0, n) in enumerate(CHUNKS):
                        s = 3 * c + ch
                        if not first or s >= 2:
                            pe.wait_ge(glu_done, i * 6 + s - 1)
                        pair_chunk(B_PW1 + 4 * c, 2 * (s % 2), 2 * (s % 2) + 1, c0, n, ch == 2
                                   ).then_inc(pw1_done, 1)

            rounds(KT // 2, pw1_round)

            pe.wait_ge(conv_done, KT)
            for again in range(2):
                for t in range(TT):
                    u = TT * again + t
                    if again and t >= 2:
                        pe.wait_ge(cn_ready, t - 1)
                    elif u >= 2:
                        pe.wait_ge(ct_read, u - 1)
                    for k in range(KT):
                        mm = pe.transpose(bank[2 * (u % 2) + k // 4][:, cols(k % 4)], conv[:, k, cols(t)],
                                          ident[:])
                    mm.then_inc(ct_turned, 1)
                    if again and t >= 1:
                        back_tile(t - 1)
            back_tile(TT - 1)

            def out_projection(base, use):
                for n in range(2):
                    for t0, t1 in BLOCKS:
                        for k in range(KT):
                            p = base + n * KT + k
                            pe.wait_ge(piece_split, p + 1)
                            for t in range(t0, t1):
                                before = bank_before(n * TT + t)
                                if k == 0 and before is not None:
                                    pe.wait_ge(proj_kept, N_PROJ * use + before + 1)
                                mm = product(bank[t % 8][:, :], xpart(k, t * P, P),
                                             (WH[:, p % RING, :], WL[:, p % RING, :]),
                                             k == 0, k == KT - 1, uses=(t == TT - 1))
                                if k == KT - 1:
                                    mm.then_inc(proj_done, 1)

            pe.wait_ge(silu_lo, TT)
            out_projection(B_PW2, 0)

            def ffn(layer, use):
                base = FFN_BASE[layer]
                f0, d0 = 3 * FT_ALL * layer, N_DOWN * layer
                pe.wait_ge(turned_lo, 2 * TT * (use + 1))

                def up_tile(p, i, s0, first):
                    for ch, (c0, n) in enumerate(CHUNKS):
                        s = s0 + ch
                        if ch == 0:
                            pe.wait_ge(piece_split, i * 24 + p + 4)
                        if not first or s >= 2:
                            pe.wait_ge(ffn_raw, f0 + s - 1 + i * 12)
                        pair_chunk(p, 2 * (s % 2), 2 * (s % 2) + 1, c0, n, ch == 2).then_inc(ffn_up, 1)

                def down_bank(p, i, m, t, n, h0, rows, first):
                    if n == 0:
                        pe.wait_ge(ffn_h, f0 + h0 + H_CHUNK[t] + 1 + i * 12)
                    if not first or m >= 4:
                        pe.wait_ge(down_kept, d0 + m - 3 + i * 40)
                    for j in range(2):
                        q = p + 2 * n + j
                        r = rows[j]
                        mm = product(bank[4 + m % 4][:, :], (HH[0:r, j, cols(t)], HL[0:r, j, cols(t)]),
                                     (WH[0:r, q % RING, :], WL[0:r, q % RING, :]),
                                     j == 0, j == 1, uses=(t == TT - 1))
                    mm.then_inc(down_done, 1)

                def two_groups(i, first):
                    for g in range(2):
                        p = base + 12 * g
                        for f in range(2):
                            up_tile(p + 4 * f, i, 6 * g + 3 * f, first)
                        for n in range(2):
                            pe.wait_ge(piece_split, i * 24 + p + 8 + 2 * n + 2)
                            for t in range(TT):
                                down_bank(p + 8, i, 20 * g + TT * n + t, t, n, 6 * g + 3, (P, P), first)

                rounds(GROUPS // 2, two_groups)
                p, s = base + 12 * GROUPS, 6 * GROUPS
                up_tile(p, 0, s, False)
                pe.wait_ge(piece_split, p + 6)
                for ch, (c0, n) in enumerate(CHUNKS):
                    pe.wait_ge(ffn_raw, f0 + s + 3 + ch - 1)
                    b = 2 * ((s + 3 + ch) % 2)
                    for k in range(KT):
                        mm = product(bank[b][:, 0:n], wblock(p + 4, k), xpart(k, c0, n),
                                     k == 0, k == KT - 1, uses=(ch == 2 and k % 4 == 3))
                    mm.then_inc(ffn_up, 1)
                pe.wait_ge(piece_split, p + 10)
                for t in range(TT):
                    for n in range(2):
                        down_bank(p + 6, 0, 20 * GROUPS + 2 * t + n, t, n, s + 3, (P, FR), False)
                    if layer + 1 < DEPTH and t >= 2:
                        pe.wait_ge(ln_ready, TT * use + t - 1)
                        turn_tile(use + 1, t - 2)
                if layer + 1 < DEPTH:
                    for t in range(TT - 2, TT):
                        pe.wait_ge(ln_ready, TT * use + t + 1)
                        turn_tile(use + 1, t)

            def turn_after_projection(use):
                for t in range(TT):
                    pe.wait_ge(ln_ready, TT * (use - 1) + t + 1)
                    if t == 0:
                        pe.wait_ge(proj_kept, N_PROJ * (1 if use == 1 else 2))
                    turn_tile(use, t)

            turn_after_projection(1)
            ffn(0, 1)

            pe.wait_ge(turned_lo, 2 * TT * 3)
            unit = 0

            def take_bank():
                if unit >= 4:
                    pe.wait_ge(qkv_kept, unit - 3)

            def channel_projection(p):
                nonlocal unit
                pe.wait_ge(piece_split, p + 2)
                for ch, (c0, n) in enumerate(CHUNKS):
                    take_bank()
                    for k in range(KT):
                        mm = product(bank[unit % 4][:, 0:n], wblock(p, k), xpart(k, c0, n),
                                     k == 0, k == KT - 1, uses=(ch == 2 and k % 4 == 3))
                    mm.then_inc(qkv_done, 1)
                    unit += 1

            for c in range(2):
                channel_projection(B_KV + 2 * c)
            pe.wait_ge(piece_split, B_KV + 8)
            for t in range(TT):
                take_bank()
                for k in range(KT):
                    q, c = (B_KV + 4 + k // 2) % RING, slice((k % 2) * KVD, (k % 2 + 1) * KVD)
                    mm = product(bank[unit % 4][:, 0:KVD], xpart(k, t * P, P), (WH[:, q, c], WL[:, q, c]),
                                 k == 0, k == KT - 1, uses=(t == TT - 1 and k % 2 == 1))
                mm.then_inc(qkv_done, 1)
                unit += 1
            for c in range(KT):
                channel_projection(B_Q + 2 * c)

            def scores(i):
                n, rr, par = ATT[i]
                kb = key_blocks(n)
                half = slice(par * HD, (par + 1) * HD)
                for r in range(GROUP):
                    u = GROUP * i + r
                    if u >= 3:
                        pe.wait_ge(score_kept, u - 2)
                    pe.matmul(bank[SCORE_BANKS[u % 3]][:, 0:len(kb) * P], q_sb[half, GROUP * rr + r, cols(n)],
                              k_sb[half, rr, kb[0] * P:(kb[-1] + 1) * P], start=True, stop=True
                              ).then_inc(score_done, 1)

            pe.wait_ge(qkv_kept, unit)
            for i in range(3):
                scores(i)
            for i, (n, rr, par) in enumerate(ATT):
                kb = key_blocks(n)
                if i >= 1:
                    pe.wait_ge(probs_T_kept, KEYS_TO[i])
                pe.wait_ge(probs_ready, i + 1)
                pe.wait_ge(probs_ready_pool, i + 1)
                for j in range(len(kb)):
                    for r in range(GROUP):
                        mm = pe.transpose(bank[2 + j][:, cols(r)], probs[:, i % 3, r, cols(j)], ident[:])
                    mm.then_inc(probs_turned, 1)
                if i + 3 < len(ATT):
                    scores(i + 3)
                if i >= 2:
                    pe.wait_ge(av_lo, i - 1)
                g = 2 * rr + par
                for j, b in enumerate(kb):
                    pe.wait_ge(probs_T_kept, KEYS_TO[i] + j + 1)
                    pe.matmul(bank[5 + i % 2][0:HD, :], v_sb[:, b, g * HD:(g + 1) * HD],
                              probsT[:, (KEYS_TO[i] + j) % 2, :], start=(j == 0), stop=(j == len(kb) - 1)
                              ).then_inc(av_done, 1)

            pe.wait_ge(av_lo, len(ATT))
            out_projection(B_O, 1)
            turn_after_projection(3)
            ffn(1, 3)

        def ffn_groups(layer):
            return 3 * FT_ALL * layer, N_DOWN * layer

        @block.scalar
        def _(act):
            def rounds(count, body):
                body(0, True)
                with act.Fori(1, count) as i:
                    body(i, False)

            for t in range(TT):
                act.dma_start(y[:, t, :], x_rows[t]).then_inc(x_landed[t], 16)
            for layer in range(DEPTH):
                for first_row, col in ((0, 0), (FT, F)):
                    for taps, src in ((slice(0, 3), w["ffn_w_dw"][layer]), (slice(3, 4), w["ffn_b_dw"][layer:layer + 1])):
                        act.dma_start(ffn_rows[first_row:first_row + FT, layer, taps, :],
                                      src[:, col:col + FT * P].rearrange("t (f p) -> f t p", p=P)
                                      ).then_inc(tables_landed, 16)
                        d0 = 0 if col == 0 else FR
                        act.dma_start(ffn_rows[2 * FT:2 * FT + 1, layer, taps, d0:d0 + FR],
                                      src[:, col + FT * P:col + F].rearrange("t (f p) -> f t p", p=FR)
                                      ).then_inc(tables_landed, 16)
            act.dma_start(conv_rows[:], w["conv_w_dw"][0]).then_inc(tables_landed, 16)
            for row, name, n in ((0, "conv_b_dw", 1), (1, "conv_norm_g", 1), (2, "conv_norm_b", 1),
                                 (3, "conv_b_pw1", 2)):
                act.dma_start(chan_rows[row * KT:(row + n) * KT, :],
                              w[name].rearrange("a (k p) -> (a k) p", p=P)).then_inc(tables_landed, 16)
            act.dma_start(sink[:], w["attn_sink"][0:1, :].to_broadcast([P, NH])).then_inc(tables_landed, 16)

            def keep_hi(use, t):
                for half in range(2):
                    b = 2 * TT * use + 2 * t + half
                    act.wait_ge(turned, b + 1)
                    act.activation(XH[:, 4 * half:4 * half + 4, cols(t)],
                                   bank[b % 4][:].rearrange("p (k t) -> p k t", t=P), ACT.Copy
                                   ).then_inc(turned_hi, 1)

            def load_gains(which, layer, bias=None):
                g, b = w[f"ln_{which}_g"], w[f"ln_{which}_b"]
                act.dma_start(gain[:], g[layer:layer + 1, :].to_broadcast([P, D])).then_inc(gains_landed, 16)
                act.dma_start(shift[:], b[layer:layer + 1, :].to_broadcast([P, D])).then_inc(gains_landed, 16)
                if bias is not None:
                    act.dma_start(pw2_bias[:], bias.to_broadcast([P, D])).then_inc(gains_landed, 16)

            def deviation(ln, t):
                act.wait_ge(var_ready, TT * ln + t + 1)
                act.activation(std[:, t:t + 1], mv[:, t, 1:2], ACT.Sqrt, bias=eps[:, 0:1]).then_inc(std_ready, 1)

            def keep_tile(use, t):
                keep_hi(use, t)
                act.activation(y[:, t, :], y[:, t, :], ACT.Copy, scale=ALPHA).then_inc(scaled, 1)

            for t in range(TT):
                keep_hi(0, t)

            act.wait_ge(tab_kept, 3)

            def pw1_round(i, first):
                for c in range(2):
                    for ch, (c0, n) in enumerate(CHUNKS):
                        s = 3 * c + ch
                        act.wait_ge(pw1_done, i * 6 + s + 1)
                        if not first or s >= 1:
                            act.wait_ge(glu_done, i * 6 + s)
                        act.sem_inc(act_passed, 1)
                        act.activation(sig[:, 0:n], bank[2 * (s % 2) + 1][:, 0:n], ACT.Sigmoid,
                                       bias=chan[:, 4, bass.ds(i * 2 + c, 1)]).then_inc(sig_ready, 1)

            rounds(KT // 2, pw1_round)
            act.wait_ge(conv_var, 1)
            act.activation(std[:, :], mv[:, :, 1], ACT.Sqrt, bias=eps[:, 0:1]).then_inc(conv_std, 1)
            for t in range(TT):
                act.wait_ge(cn_turned, t + 1)
                if t >= 2:
                    act.wait_ge(silu_lo, t - 1)
                for k in range(KT):
                    ins = act.activation(act_out[:, t % 2, k, :], bank[4 + 2 * (t % 2) + k // 4][:, cols(k % 4)],
                                         ACT.Silu, bias=chan[:, 2, k:k + 1], scale=chan[:, 1, k:k + 1])
                ins.then_inc(silu_ready, 1)
                act.wait_ge(silu_ready, t + 1)
                act.activation(XH[:, :, cols(t)], act_out[:, t % 2, :, :], ACT.Copy).then_inc(silu_hi, 1)
            for t in range(TT):
                act.dma_start(y[:, t, :], x_rows[t]).then_inc(res_landed[t], 16)
            load_gains("mix", 0, w["conv_b_pw2"][0:1, :])
            for t in range(TT):
                deviation(0, t)
            for t in range(TT):
                keep_tile(1, t)

            def ffn(layer, use):
                f0, _ = ffn_groups(layer)
                act.wait_ge(ln_ready, TT * use)
                load_gains("ffn", layer)

                def chunk(i, s, ch, first, narrow=False):
                    n, col = CHUNKS[ch][1], RAW_COL[ch]
                    act.wait_ge(ffn_up, f0 + s + 1 + i * 12)
                    if not first or s >= 3:
                        act.wait_ge(ffn_conv, f0 + s - (1 if ch == 0 else 2) + i * 12)
                    for part in range(1 if narrow else 2):
                        ins = act.activation(gu_raw[:, part, col:col + n], bank[2 * (s % 2) + part][:, 0:n],
                                             ACT.Copy)
                    ins.then_inc(ffn_raw, 1)
                    act.wait_ge(ffn_gc, f0 + s + 1 + i * 12)
                    n, rows = CONV_CHUNKS[ch][1], FR if narrow else P
                    act.activation(g_conv[0:rows, 0:n], g_conv[0:rows, 0:n], ACT.Silu).then_inc(ffn_silu, 1)

                def two_groups(i, first):
                    for s in range(12):
                        chunk(i, s, s % 3, first)

                rounds(GROUPS // 2, two_groups)
                for s in range(6 * GROUPS, 6 * GROUPS + 6):
                    chunk(0, s, s % 3, False, narrow=s >= 6 * GROUPS + 3)
                if layer + 1 < DEPTH:
                    for t in range(TT):
                        deviation(use, t)
                        if t >= 2:
                            keep_hi(use + 1, t - 2)
                    for t in range(TT - 2, TT):
                        keep_hi(use + 1, t)
                    for t in range(TT):
                        act.dma_start(residual_rows[t], y[:, t, :]).then_inc(res_stored, 16)
                else:
                    for t in range(TT):
                        deviation(use, t)
                        if t >= 1:
                            act.wait_ge(ln_ready, TT * use + t)
                            act.dma_start(out_rows[t - 1], y[:, t - 1, :]).then_inc(out_stored, 16)
                    act.wait_ge(ln_ready, TT * use + TT)
                    act.dma_start(out_rows[TT - 1], y[:, TT - 1, :]).then_inc(out_stored, 16)
                    act.wait_ge(out_stored, 16 * TT)

            ffn(0, 1)

            unit = 0

            def keep(out, n, scale=1.0):
                nonlocal unit
                act.wait_ge(qkv_done, unit + 1)
                act.activation(out, bank[unit % 4][:, 0:n], ACT.Copy, scale=scale).then_inc(qkv_kept, 1)
                unit += 1

            for c in range(2):
                for c0, n in CHUNKS:
                    keep(k_sb[:, c, c0:c0 + n], n)
            for t in range(TT):
                keep(v_sb[:, t, :], KVD)
            act.wait_ge(res_stored, 16 * TT)
            for c in range(KT):
                for c0, n in CHUNKS:
                    keep(q_sb[:, c, c0:c0 + n], n, scale=HD ** -0.5)

            def exponentials(i):
                n, rr, par = ATT[i]
                nk, b = len(key_blocks(n)) * P, i % 3
                act.wait_ge(max_ready, i + 1)
                for r in range(GROUP):
                    act.activation(probs[:, b, r, 0:nk], probs[:, b, r, 0:nk], ACT.Exp,
                                   bias=nmax[:, b, r:r + 1], accum_out=ssum[:, b, r:r + 1])
                act.activation(sexp[:, b, :], sexp[:, b, :], ACT.Exp).then_inc(exp_ready, 1)

            for i in range(3):
                exponentials(i)
            for i, (n, rr, par) in enumerate(ATT):
                for j in range(len(key_blocks(n))):
                    u = KEYS_TO[i] + j
                    act.wait_ge(probs_turned, u + 1)
                    if u >= 2:
                        act.wait_ge(av_done, u - 1)
                    act.activation(probsT[:, u % 2, :], bank[2 + j][:, :], ACT.Copy).then_inc(probs_T_kept, 1)
                act.wait_ge(av_done, KEYS_TO[i + 1])
                act.activation(XH[par * HD:(par + 1) * HD, GROUP * rr:GROUP * (rr + 1), cols(n)],
                               bank[5 + i % 2][0:HD, :].rearrange("p (k t) -> p k t", t=P), ACT.Copy
                               ).then_inc(av_hi, 1)
                if i + 3 < len(ATT):
                    exponentials(i + 3)
            act.wait_ge(av_lo, len(ATT))
            for t in range(TT):
                act.dma_start(y[:, t, :], residual_rows[t]).then_inc(res_landed[t], 16)
            load_gains("mix", 1)
            for t in range(TT):
                deviation(2, t)
            for t in range(TT):
                keep_tile(3, t)
            ffn(1, 3)

        @block.vector
        def _(dve):
            vs = Count()

            def keep_lo(use, t):
                for half in range(2):
                    b = 2 * TT * use + 2 * t + half
                    dve.wait_ge(turned_hi, b + 1)
                    k = slice(4 * half, 4 * half + 4)
                    dve.tensor_tensor(XL[:, k, cols(t)], bank[b % 4][:].rearrange("p (k t) -> p k t", t=P),
                                      XH[:, k, cols(t)].bitcast(F32), ALU.subtract).then_inc(turned_lo, 1)

            def norm_stats(ln, t, written):
                dve.wait_ge(*written)
                for half in range(2):
                    dve.bn_stats(stats[:, t % 2, half, :], y[:, t, half * HALF:(half + 1) * HALF]
                                 ).then_inc(vec_step, vs.one())
                dve.wait_ge(vec_step, vs.now())
                dve.bn_aggr(mv[:, t, :], stats[:, t % 2, :, :]).then_inc(var_ready, 1)

            def norm_apply(ln, t):
                dve.wait_ge(std_ready, TT * ln + t + 1)
                dve.reciprocal(rstd[:, t:t + 1], std[:, t:t + 1]).then_inc(vec_step, vs.one())
                dve.wait_ge(vec_step, vs.now())
                dve.wait_ge(var_ready, TT * ln + t + 1)
                dve.tensor_scalar(y[:, t, :], y[:, t, :], mv[:, t, 0:1], rstd[:, t:t + 1], ALU.subtract,
                                  ALU.mult).then_inc(vec_step, vs.one())
                dve.wait_ge(gains_landed, GAINS_BY[ln])
                dve.wait_ge(vec_step, vs.now())
                dve.tensor_tensor(y[:, t, :], y[:, t, :], gain[:], ALU.mult).then_inc(vec_step, vs.one())
                dve.wait_ge(vec_step, vs.now())
                dve.tensor_tensor(y[:, t, :], y[:, t, :], shift[:], ALU.add).then_inc(ln_ready, 1)

            for t in range(TT):
                keep_lo(0, t)
            dve.wait_ge(tab_turned, 1)
            dve.tensor_copy(ffn_tab[:].rearrange("p l t c -> p (l t c)"), bank[4][:, 0:4 * DEPTH * CONV_COLS]
                            ).then_inc(tab_kept, 1)
            dve.wait_ge(tab_turned, 2)
            dve.tensor_copy(conv_tab[:].rearrange("p k t -> p (k t)"), bank[5][:, 0:KT * TAPS]).then_inc(tab_kept, 1)
            dve.wait_ge(tab_turned, 3)
            dve.tensor_copy(chan[:].rearrange("p v k -> p (v k)"), bank[6][:, 0:5 * KT]).then_inc(tab_kept, 1)
            dve.memset(glu[:], 0.0).then_inc(vec_step, vs.one())
            dve.wait_ge(vec_step, vs.now())
            dve.wait_ge(tab_kept, 3)

            GLU_COL = [PAD, PAD + HALF, PAD + S0 + PAD]
            LONG = S0 + PAD + S1

            def conv_round(i, first):
                for c in range(2):
                    for ch, (c0, n) in enumerate(CHUNKS):
                        s = 3 * c + ch
                        dve.wait_ge(sig_ready, i * 6 + s + 1)
                        dve.scalar_tensor_tensor(
                            out=glu[:, GLU_COL[ch]:GLU_COL[ch] + n], in0=bank[2 * (s % 2)][:, 0:n],
                            scalar=chan[:, 3, bass.ds(i * 2 + c, 1)], in1=sig[:, 0:n],
                            op0=ALU.add, op1=ALU.mult).then_inc(glu_done, 1)
                    dve.wait_ge(glu_done, i * 6 + 3 * c + 3)
                    tap = lambda k: conv_tab[:, bass.ds(i * 2 + c, 1), k]
                    dve.tensor_scalar(acc[:], glu[:, 0:LONG], tap(0), chan[:, 0, bass.ds(i * 2 + c, 1)],
                                      ALU.mult, ALU.add).then_inc(vec_step, vs.one())
                    for k in range(1, TAPS - 1):
                        dve.wait_ge(vec_step, vs.now())
                        dve.scalar_tensor_tensor(out=acc[:], in0=glu[:, k:k + LONG], scalar=tap(k), in1=acc[:],
                                                 op0=ALU.mult, op1=ALU.add).then_inc(vec_step, vs.one())
                    dve.wait_ge(vec_step, vs.now())
                    k = TAPS - 1
                    for c0, n, a0 in ((0, S0, 0), (S0, S1, S0 + PAD)):
                        ins = dve.scalar_tensor_tensor(
                            out=conv[:, bass.ds(i * 2 + c, 1), c0:c0 + n], in0=glu[:, a0 + k:a0 + k + n],
                            scalar=tap(k), in1=acc[:, a0:a0 + n], op0=ALU.mult, op1=ALU.add)
                    ins.then_inc(conv_done, 1)
                    dve.wait_ge(conv_done, i * 2 + c + 1)

            vs.rounds(dve, KT // 2, conv_round)

            for t in range(TT):
                dve.wait_ge(ct_turned, t + 1)
                dve.bn_stats(stats[:, t % 2, 0, :], bank[2 * (t % 2)][:]).then_inc(vec_step, vs.one())
                dve.bn_stats(stats[:, t % 2, 1, :], bank[2 * (t % 2) + 1][:]).then_inc(ct_read, 1)
                dve.wait_ge(vec_step, vs.now())
                dve.wait_ge(ct_read, t + 1)
                dve.bn_aggr(mv[:, t, :], stats[:, t % 2, :, :]).then_inc(vec_step, vs.one())
            dve.wait_ge(vec_step, vs.now())
            dve.engine_nop().then_inc(conv_var, 1)
            dve.wait_ge(conv_std, 1)
            dve.reciprocal(rstd[:], std[:]).then_inc(vec_step, vs.one())
            dve.wait_ge(vec_step, vs.now())

            def silu_low(t):
                dve.wait_ge(silu_hi, t + 1)
                dve.tensor_tensor(XL[:, :, cols(t)], act_out[:, t % 2, :, :], XH[:, :, cols(t)].bitcast(F32),
                                  ALU.subtract).then_inc(silu_lo, 1)

            for t in range(TT):
                dve.wait_ge(ct_turned, TT + t + 1)
                if t >= 2:
                    dve.wait_ge(cn_turned, t - 1)
                for half in range(2):
                    ins = dve.tensor_scalar(normed[:, t % 2, half * HALF:(half + 1) * HALF],
                                            bank[2 * (t % 2) + half][:], mv[:, t, 0:1], rstd[:, t:t + 1],
                                            ALU.subtract, ALU.mult)
                ins.then_inc(cn_ready, 1)
                if t >= 1:
                    silu_low(t - 1)
            silu_low(TT - 1)

            def out_projection(use, ln, biased):
                for n in range(2):
                    for t in range(TT):
                        m = n * TT + t
                        if n == 0:
                            dve.wait_ge(res_landed[t], 16 * (use + 1))
                        dve.wait_ge(proj_done, N_PROJ * use + m + 1)
                        half = slice(n * HALF, (n + 1) * HALF)
                        dve.scalar_tensor_tensor(out=y[:, t, half], in0=y[:, t, half], scalar=ALPHA,
                                                 in1=bank[t % 8][:], op0=ALU.mult, op1=ALU.add
                                                 ).then_inc(proj_kept, 1)
                        if n == 0:
                            continue
                        written = (proj_kept, N_PROJ * use + m + 1)
                        if biased:
                            dve.wait_ge(gains_landed, GAINS_BY[ln])
                            dve.wait_ge(*written)
                            dve.tensor_tensor(y[:, t, :], y[:, t, :], pw2_bias[:], ALU.add
                                              ).then_inc(vec_step, vs.one())
                            written = (vec_step, vs.now())
                        norm_stats(ln, t, written)
                        if t >= 1:
                            norm_apply(ln, t - 1)
                norm_apply(ln, TT - 1)
                for t in range(TT):
                    keep_lo(ln + 1, t)

            def ffn(layer, use):
                f0, d0 = ffn_groups(layer)
                for col in (0, 1 + S0, 1 + S0 + 1 + S1):
                    dve.memset(gu_raw[:, :, col:col + 1], 0.0).then_inc(vec_step, vs.one())
                dve.wait_ge(vec_step, vs.now())

                def conv3(out, part, ch, col, last_sem, rows=P):
                    _, n, a0 = CONV_CHUNKS[ch]
                    tab = lambda tap: ffn_tab[:, layer, tap, col]
                    dve.tensor_scalar(out[:, 0:n], gu_raw[:, part, a0:a0 + n], tab(0), tab(3), ALU.mult,
                                      ALU.add).then_inc(vec_step, vs.one())
                    for tap in (1, 2):
                        dve.wait_ge(vec_step, vs.now())
                        ins = dve.scalar_tensor_tensor(
                            out=out[:, 0:n], in0=gu_raw[:, part, a0 + tap:a0 + tap + n], scalar=tab(tap),
                            in1=out[:, 0:n], op0=ALU.mult, op1=ALU.add)
                        if tap == 1:
                            ins.then_inc(vec_step, vs.one())
                    ins.then_inc(last_sem, 1)

                def split_hidden(i, s, ch, slot, rows):
                    c0, n, _ = CONV_CHUNKS[ch]
                    dve.wait_ge(ffn_silu, f0 + s + 1 + i * 12)
                    dve.wait_ge(ffn_conv, f0 + s + 1 + i * 12)
                    u, hi, lo = u_conv[0:rows, 0:n], HH[0:rows, slot, c0:c0 + n], HL[0:rows, slot, c0:c0 + n]
                    dve.tensor_tensor(u, g_conv[0:rows, 0:n], u, ALU.mult).then_inc(vec_step, vs.one())
                    dve.wait_ge(vec_step, vs.now())
                    dve.tensor_copy(hi, u).then_inc(vec_step, vs.one())
                    dve.wait_ge(vec_step, vs.now())
                    dve.tensor_tensor(lo, u, hi.bitcast(F32), ALU.subtract).then_inc(ffn_h, 1)
                    dve.wait_ge(ffn_h, f0 + s + 1 + i * 12)

                def chunk(i, s, ch, slot, f, group_done):
                    dve.wait_ge(ffn_raw, f0 + s + 1 + i * 12)
                    conv3(g_conv, 0, ch, bass.ds(i * 4 + f, 1), ffn_gc)
                    conv3(u_conv, 1, ch, bass.ds(i * 4 + FT + f, 1), ffn_conv)
                    if group_done is not None:
                        dve.wait_ge(down_done, group_done)
                    split_hidden(i, s, ch, slot, P)

                def add_down(i, m, t, n):
                    dve.wait_ge(down_done, d0 + m + 1 + i * 40)
                    half = slice(n * HALF, (n + 1) * HALF)
                    dve.tensor_tensor(y[:, t, half], y[:, t, half], bank[4 + m % 4][:], ALU.add
                                      ).then_inc(down_kept, 1)

                def two_groups(i, first):
                    for g in range(2):
                        for f in range(2):
                            for ch in range(3):
                                done = None if first and g == 0 else d0 + 20 * g + i * 40
                                chunk(i, 6 * g + 3 * f + ch, ch, f, 2 * g + f, done)
                        if first and g == 0:
                            dve.wait_ge(scaled, TT * (layer + 1))
                        for n in range(2):
                            for t in range(TT):
                                add_down(i, 20 * g + TT * n + t, t, n)

                vs.rounds(dve, GROUPS // 2, two_groups)
                s = 6 * GROUPS
                for ch in range(3):
                    chunk(0, s + ch, ch, 0, FT - 1, d0 + 20 * GROUPS)
                for ch in range(3):
                    n = CONV_CHUNKS[ch][1]
                    dve.wait_ge(ffn_raw, f0 + s + 3 + ch + 1)
                    conv3(g_conv, 0, ch, slice(2 * FT, 2 * FT + 1), ffn_conv)
                    dve.wait_ge(ffn_conv, f0 + s + 3 + ch + 1)
                    dve.tensor_copy(u_conv[0:FR, 0:n], g_conv[FR:P, 0:n]).then_inc(ffn_gc, 1)
                    dve.wait_ge(ffn_gc, f0 + s + 3 + ch + 1)
                    split_hidden(0, s + 3 + ch, ch, 1, FR)
                turning = layer + 1 < DEPTH
                for t in range(TT):
                    for n in range(2):
                        add_down(0, 20 * GROUPS + 2 * t + n, t, n)
                    norm_stats(use, t, (down_kept, d0 + 20 * GROUPS + 2 * t + 2))
                    if t >= 1:
                        norm_apply(use, t - 1)
                    if turning and t >= 3:
                        keep_lo(use + 1, t - 3)
                norm_apply(use, TT - 1)
                for t in range(TT - 3, TT):
                    if turning:
                        keep_lo(use + 1, t)

            out_projection(0, 0, True)
            ffn(0, 1)

            dve.wait_ge(tables_landed, 16 * N_TABLE_DMAS)
            dve.wait_ge(consts_ready, 3)
            dve.scalar_tensor_tensor(out=dist[:], in0=dist[:], scalar=-1.0, in1=dist[:], op0=ALU.mult,
                                     op1=ALU.max).then_inc(vec_step, vs.one())
            dve.wait_ge(vec_step, vs.now())

            def biased_scores(i):
                n, rr, par = ATT[i]
                kb = key_blocks(n)
                nk, d0, b = len(kb) * P, (kb[0] - n + 1) * P, i % 3
                h0 = GROUP * (2 * rr + par)
                if i >= 3:
                    dve.wait_ge(probs_turned, KEYS_TO[i - 2])
                for r in range(GROUP):
                    u = GROUP * i + r
                    dve.wait_ge(score_done, u + 1)
                    dve.scalar_tensor_tensor(out=probs[:, b, r, 0:nk], in0=dist[:, d0:d0 + nk],
                                             scalar=-SLOPES[h0 + r], in1=bank[SCORE_BANKS[u % 3]][:, 0:nk],
                                             op0=ALU.mult, op1=ALU.add).then_inc(score_kept, 1)
                dve.wait_ge(score_kept, GROUP * (i + 1))
                dve.tensor_reduce(nmax[:, b, :], probs[:, b, :, 0:nk], AX_X, ALU.max).then_inc(vec_step, vs.one())
                dve.wait_ge(vec_step, vs.now())
                dve.tensor_tensor(nmax[:, b, :], nmax[:, b, :], sink[:, h0:h0 + GROUP], ALU.max
                                  ).then_inc(vec_step, vs.one())
                dve.wait_ge(vec_step, vs.now())
                dve.tensor_scalar(nmax[:, b, :], nmax[:, b, :], -1.0, None, ALU.mult).then_inc(vec_step, vs.one())
                dve.wait_ge(vec_step, vs.now())
                dve.tensor_tensor(sexp[:, b, :], nmax[:, b, :], sink[:, h0:h0 + GROUP], ALU.add
                                  ).then_inc(max_ready, 1)

            def normalise(i):
                n, rr, par = ATT[i]
                nk, b = len(key_blocks(n)) * P, i % 3
                dve.wait_ge(exp_ready, i + 1)
                if i >= 3:
                    dve.wait_ge(probs_ready_pool, i - 2)
                dve.tensor_tensor(ssum[:, b, :], ssum[:, b, :], sexp[:, b, :], ALU.add).then_inc(vec_step, vs.one())
                dve.wait_ge(vec_step, vs.now())
                dve.reciprocal(srec[:, b, :], ssum[:, b, :]).then_inc(recip_ready, 1)
                dve.wait_ge(recip_ready, i + 1)
                for r in range(GROUP // 2):
                    ins = dve.tensor_scalar(probs[:, b, r, 0:nk], probs[:, b, r, 0:nk], srec[:, b, r:r + 1],
                                            None, ALU.mult)
                ins.then_inc(probs_ready, 1)

            def heads_low(i):
                n, rr, par = ATT[i]
                dve.wait_ge(av_hi, i + 1)
                where = slice(par * HD, (par + 1) * HD), slice(GROUP * rr, GROUP * (rr + 1)), cols(n)
                dve.tensor_tensor(XL[where], bank[5 + i % 2][0:HD, :].rearrange("p (k t) -> p k t", t=P),
                                  XH[where].bitcast(F32), ALU.subtract).then_inc(av_lo, 1)

            for i in range(3):
                biased_scores(i)
            normalise(0)
            for i in range(len(ATT)):
                if i + 1 < len(ATT):
                    normalise(i + 1)
                if i + 3 < len(ATT):
                    biased_scores(i + 3)
                if i >= 1:
                    heads_low(i - 1)
            heads_low(len(ATT) - 1)
            out_projection(1, 2, False)
            ffn(1, 3)


_INS = ["x_prompt", "x_sample", "conv_w_pw1", "conv_b_pw1", "conv_w_dw", "conv_b_dw", "conv_norm_g",
        "conv_norm_b", "conv_w_pw2", "conv_b_pw2", "attn_w_q", "attn_w_kv", "attn_w_o", "attn_sink",
        "ffn_w_up", "ffn_w_dw", "ffn_b_dw", "ffn_w_down", "ln_mix_g", "ln_mix_b", "ln_ffn_g", "ln_ffn_b"]


def kernel(**inputs):
    import numpy as _np
    import concourse.bacc as _bacc
    from concourse import mybir as _mybir
    from concourse.bass_utils import run_bass_kernel_spmd as _run

    nc = _bacc.Bacc("TRN2", target_bir_lowering=False, num_devices=1)
    arrays, weights = {}, {}
    for name in _INS:
        a = _np.ascontiguousarray(inputs[name])
        arrays[f"in_{name}_dram"] = a
        weights[name] = nc.dram_tensor(f"in_{name}_dram", a.shape, _mybir.dt.from_np(a.dtype),
                                       kind="ExternalInput").ap()
    f32 = _mybir.dt.float32
    prompt, sample = inputs["x_prompt"].shape, inputs["x_sample"].shape
    out0 = nc.dram_tensor("out_0_dram", prompt, f32, kind="ExternalOutput").ap()
    out1 = nc.dram_tensor("out_1_dram", sample, f32, kind="ExternalOutput").ap()
    residual = nc.dram_tensor("residual_dram", (prompt[1] + sample[1], prompt[2]), f32, kind="Internal").ap()
    trunk(nc, weights, out0, out1, residual)
    r = _run(nc, [arrays], core_ids=[0])
    return r.results[0]["out_0_dram"], r.results[0]["out_1_dram"]
```

```python
from contextlib import ExitStack

import concourse.bass as bass
from concourse import mybir

F32 = mybir.dt.float32
F32R = mybir.dt.float32r
I32 = mybir.dt.int32
ALU = mybir.AluOpType
ACT = mybir.ActivationFunctionType
AX_X = mybir.AxisListType.X

P = 128
HALF = 512
RAW = 4
RING = 8


class Count:

    def __init__(self):
        self.n = 0
        self.loop = 0
        self.start = 0

    def one(self):
        self.n += 1
        return 1

    def now(self):
        return self.loop + self.n

    def rounds(self, engine, count, body, per_round):
        body(0, True)
        before = self.n
        with engine.Fori(1, count) as i:
            self.loop = i * per_round - per_round
            body(i, False)
        assert self.n == before + per_round, (self.n - before, per_round)
        self.n, self.loop = before + (count - 1) * per_round, 0


def trunk(nc, w, out_prompt, out_sample, residual_dram):
    D = w["x_prompt"].shape[2]
    S0, S1 = w["x_prompt"].shape[1], w["x_sample"].shape[1]
    T = S0 + S1
    TT = T // P
    KT = D // P
    T0 = S0 // P
    TAPS = w["conv_w_dw"].shape[1]
    PAD = TAPS // 2
    NKV = 4
    NH = w["attn_sink"].shape[1]
    GROUP = NH // NKV
    HD = D // NH
    KVD = NKV * HD
    F = w["ffn_w_down"].shape[1]
    FT = F // P
    FR = F - FT * P
    DEPTH = w["ffn_w_up"].shape[0]
    NORMS = 2 * DEPTH - 1
    PE_TAPS = 9
    MORE_TAPS = 13
    ALPHA = (2.0 * DEPTH) ** 0.25
    EPS = 1e-5
    SLOPES = [2.0 ** (-8.0 * (h + 1) / NH) for h in range(NH)]
    FAR = 1.0e35
    CHUNKS = [(0, HALF), (HALF, HALF), (S0, S1)]
    assert S0 == 2 * HALF and S1 <= HALF and FR == 64 and D == 2 * HALF and HD == 64
    GROUPS = (FT - 1) // 2
    assert 2 * GROUPS + 1 == FT and GROUPS % 2 == 0
    CONV_COLS = 2 * FT + 1

    UNIT = 2
    B_PW1 = 0
    B_PW2 = B_PW1 + 2 * KT * UNIT
    B_FFN0 = B_PW2 + 2 * KT
    N_FFN = GROUPS * 12 + 10
    B_KV = B_FFN0 + N_FFN
    B_Q = B_KV + 8
    B_O = B_Q + KT * UNIT
    B_FFN1 = B_O + 2 * KT
    N_PIECES = B_FFN1 + N_FFN
    FFN_BASE = [B_FFN0, B_FFN1]

    with ExitStack() as ctx:
        def sb(name, shape, dt=F32, where=ctx):
            return where.enter_context(nc.sbuf_tensor(name, shape, dt))

        def sem(name):
            return ctx.enter_context(nc.semaphore(name))

        XH = sb("x_hi", [P, KT, T], F32R)
        XL = sb("x_lo", [P, KT, T], F32R)
        y = sb("y", [P, TT, D])
        raw = sb("raw_pieces", [P, RAW, HALF])
        WH = sb("w_hi", [P, RING, HALF], F32R)
        WL = sb("w_lo", [P, RING, HALF], F32R)
        ident = sb("ident", [P, P])
        ffn_tab = sb("ffn_conv_table", [P, DEPTH, 4, CONV_COLS])
        conv_tab = sb("conv_table", [P, KT, TAPS])
        chan = sb("channel_table", [P, 5 + 2 * NORMS, KT])
        stats = sb("stats", [P, 2, 2, 6])
        mv = sb("mean_var", [P, TT, 2])
        std = sb("std", [P, TT])
        rstd = sb("rstd", [P, TT])
        eps = sb("eps", [P, 1])
        dist = sb("distance", [P, 3 * P])
        sink = sb("sink_rows", [P, NH])
        with ExitStack() as a:
            WIDE = PAD + S0 + PAD + S1 + PAD
            glu = sb("glu", [P, 2, WIDE], where=a)
            glu_hi = sb("glu_hi", [P, WIDE], F32R, where=a)
            glu_lo = sb("glu_lo", [P, WIDE], F32R, where=a)
            acc = sb("conv_acc", [P, 2, S0 + PAD + S1], where=a)
            diag = sb("tap_diagonals", [P, 2, PE_TAPS, P], F32R, where=a)
            tap_hi = sb("tap_hi", [P, KT, PE_TAPS], F32R, where=a)
            tap_lo = sb("tap_lo", [P, KT, PE_TAPS], where=a)
            more_hi = sb("more_tap_hi", [P, MORE_TAPS], F32R, where=a)
            more_lo = sb("more_tap_lo", [P, MORE_TAPS], where=a)
        with ExitStack() as a:
            normed = sb("conv_normed", [P, TT, D], where=a)
        with ExitStack() as a:
            ffn_rows = sb("ffn_rows", [CONV_COLS, DEPTH, 4, P], where=a)
            conv_rows = sb("conv_rows", [TAPS, D], where=a)
            chan_rows = sb("chan_rows", [(5 + 2 * NORMS) * KT, P], where=a)
            dist_i = sb("distance_int", [P, 3 * P], I32, where=a)
        with ExitStack() as a:
            gain = sb("gain_rows", [P, D], where=a)
            shift = sb("shift_rows", [P, D], where=a)
            HH = sb("h_hi", [P, 2, T], F32R, where=a)
            HL = sb("h_lo", [P, 2, T], F32R, where=a)
            gu_raw = sb("gate_up_raw", [P, 2, 1 + S0 + 1 + S1 + 1], where=a)
            g_conv = sb("gate_conv", [P, HALF + 1], where=a)
            u_conv = sb("up_conv", [P, HALF + 1], where=a)
        with ExitStack() as a:
            sb("gain_below", [P, D], where=a)
            sb("shift_below", [P, D], where=a)
            pw2_bias = sb("pw2_bias_rows", [P, D], where=a)
        with ExitStack() as a:
            sb("below_first", [P, 2 * D + T], where=a)
            scaled_tile = [sb("gained_tile0", [P, KT, P], where=a)]
            sb("below_second", [P, 2 * T - D], where=a)
            scaled_tile.append(sb("gained_tile1", [P, KT, P], where=a))
        with ExitStack() as a:
            scaled_end = [sb(f"gained_end{i}", [P, KT, P], where=a) for i in range(2)]
        with ExitStack() as a:
            probs = sb("probs", [P, 3, GROUP, 3 * P], where=a)
            v_sb = sb("v", [P, TT, KVD], where=a)
            k_sb = sb("k", [P, NKV // 2, T], where=a)
            probsT = sb("probs_T", [P, 2, GROUP * P], where=a)
            nmax = sb("minus_max", [P, 3, GROUP], where=a)
            sexp = sb("sink_exp", [P, 3, GROUP], where=a)
            ssum = sb("exp_sum", [P, 3, GROUP], where=a)
            srec = sb("one_over_denominator", [P, 3, GROUP], where=a)
        conv = y[:].rearrange("p t d -> p (t d)").rearrange("p (k t) -> p k t", k=KT)
        act_out = y[:, TT - 2:TT, :].rearrange("p b (k t) -> p b k t", t=P)
        q_sb = conv

        bank = [ctx.enter_context(nc.psum_tensor(f"bank{i}", [P, HALF], F32)) for i in range(8)]

        raw_landed = [sem(f"raw_landed{i}") for i in range(RAW)]
        piece_hi = sem("piece_hi")
        piece_split = sem("piece_split")
        piece_used = sem("piece_used")
        x_landed = [sem(f"x_landed{i}") for i in range(TT)]
        tables_landed = sem("tables_landed")
        consts_ready = sem("consts_ready")
        pool_step = sem("pool_step")
        pool_passed = sem("pool_passed")
        tab_turned = sem("tables_turned")
        tab_kept = sem("tables_kept")
        vec_step = sem("vec_step")
        act_passed = sem("act_passed")
        turned = sem("tile_turned")
        turned_hi = sem("turned_hi")
        turned_lo = sem("turned_lo")
        pw1_done = sem("pw1_done")
        sig_ready = sem("sig_ready")
        glu_done = sem("glu_done")
        glu_hi_ready = sem("glu_hi_ready")
        glu_lo_ready = sem("glu_lo_ready")
        diag_ready = sem("diagonals_ready")
        taps_done = sem("taps_done")
        acc_ready = sem("acc_ready")
        conv_done = sem("conv_done")
        ct_turned = sem("conv_tile_turned")
        ct_kept = sem("conv_tile_kept")
        cn_ready = sem("conv_normed_ready")
        cn_turned = sem("conv_normed_turned")
        silu_ready = sem("silu_ready")
        silu_hi = sem("silu_hi")
        silu_lo = sem("silu_lo")
        std_ready = sem("std_ready")
        conv_var = sem("conv_variances_ready")
        conv_std = sem("conv_deviations_ready")
        var_ready = sem("var_ready")
        gains_landed = sem("gains_landed")
        bias_landed = sem("bias_landed")
        ln_ready = sem("ln_ready")
        gained = sem("gained")
        gains_ready = sem("gains_ready")
        res_step = sem("residual_step")
        residual_done = sem("residual_done")
        residual_pool = sem("residual_pool")
        out_gained = sem("out_gained")
        inverse_ready = sem("inverse_ready")
        out_normed = sem("out_normed")
        out_ready = sem("out_ready")
        out_stored = sem("out_stored")
        res_stored = sem("residual_stored")
        res_landed = [sem(f"res_landed{i}") for i in range(TT)]
        proj_done = sem("proj_done")
        proj_kept = sem("proj_kept")
        ffn_up = sem("ffn_up_done")
        ffn_raw = sem("ffn_raw_kept")
        ffn_conv = sem("ffn_conv_done")
        ffn_gc = sem("ffn_gate_ready")
        ffn_silu = sem("ffn_silu_ready")
        ffn_h = sem("ffn_h_ready")
        down_done = sem("ffn_down_done")
        down_kept = sem("ffn_down_kept")
        qkv_done = sem("qkv_done")
        qkv_kept = sem("qkv_kept")
        score_done = sem("score_done")
        score_kept = sem("score_kept")
        max_ready = sem("max_ready")
        exp_ready = sem("exp_ready")
        recip_ready = sem("recip_ready")
        probs_ready = sem("probs_ready")
        probs_ready_pool = sem("probs_ready_pool")
        probs_turned = sem("probs_turned")
        probs_T_kept = sem("probs_T_kept")
        av_done = sem("av_done")
        av_hi = sem("av_hi")
        av_lo = sem("av_lo")

        block = ctx.enter_context(nc.Block())

        x_rows = [w["x_prompt"][0, t * P:(t + 1) * P, :] for t in range(T0)] + \
                 [w["x_sample"][0, t * P:(t + 1) * P, :] for t in range(TT - T0)]
        out_rows = [out_prompt[0, t * P:(t + 1) * P, :] for t in range(T0)] + \
                   [out_sample[0, t * P:(t + 1) * P, :] for t in range(TT - T0)]
        residual_rows = [residual_dram[t * P:(t + 1) * P, :] for t in range(TT)]

        def cols(t):
            return slice(t * P, (t + 1) * P)

        def norm_vectors(ln):
            which, layer = ("mix", "ffn")[ln % 2], ln // 2
            return w[f"ln_{which}_g"][layer:layer + 1, :], w[f"ln_{which}_b"][layer:layer + 1, :]

        transfers = [1] * N_PIECES
        for p in [*range(B_Q, B_FFN1), *(b + 12 * GROUPS + 4 + h for b in FFN_BASE for h in range(2))]:
            transfers[p] = 2

        def landed(p):
            return 16 * sum(transfers[p % RAW:p + 1:RAW])

        @block.sync
        def _(sp):
            def slot_free(p, earlier=0):
                if p >= RAW:
                    sp.wait_ge(piece_split, earlier + p - RAW + 1)

            def column_piece(p, mat, col, half, n=4, width=P, earlier=0):
                view = mat.rearrange("(k p) f -> p k f", p=P)
                slot_free(p, earlier)
                sp.dma_start(raw[:, p % RAW, :].rearrange("p (k f) -> p k f", f=width),
                             view[:, n * half:n * (half + 1), bass.ds(col, width)]
                             ).then_inc(raw_landed[p % RAW], 16)

            def paired_piece(p, view, half):
                slot_free(p)
                for s in range(2):
                    dst = raw[:, p % RAW, :].rearrange("p (k s f) -> p k s f", k=4, s=2)
                    sp.dma_start(dst[:, :, s, :], view[:, 4 * half:4 * half + 4, s, :]
                                 ).then_inc(raw_landed[p % RAW], 16)

            def row_piece(p, rows, earlier=0, height=P):
                slot_free(p, earlier)
                sp.dma_start(raw[0:height, p % RAW, :], rows).then_inc(raw_landed[p % RAW], 16)

            for p in range(RAW):
                column_piece(B_PW1 + p, w["conv_w_pw1"][0], (p // 2 % 2) * D + (p // 4) * P, p % 2)
            for layer in range(DEPTH):
                for first_row, col in ((0, 0), (FT, F)):
                    for taps, src in ((slice(0, 3), w["ffn_w_dw"][layer]), (slice(3, 4), w["ffn_b_dw"][layer:layer + 1])):
                        sp.dma_start(ffn_rows[first_row:first_row + FT, layer, taps, :],
                                      src[:, col:col + FT * P].rearrange("t (f p) -> f t p", p=P)
                                      ).then_inc(tables_landed, 16)
                        d0 = 0 if col == 0 else FR
                        sp.dma_start(ffn_rows[2 * FT:2 * FT + 1, layer, taps, d0:d0 + FR],
                                      src[:, col + FT * P:col + F].rearrange("t (f p) -> f t p", p=FR)
                                      ).then_inc(tables_landed, 16)
            sp.dma_start(conv_rows[:], w["conv_w_dw"][0]).then_inc(tables_landed, 16)
            for row, name, n in ((0, "conv_b_dw", 1), (1, "conv_norm_g", 1), (2, "conv_norm_b", 1),
                                 (3, "conv_b_pw1", 2)):
                sp.dma_start(chan_rows[row * KT:(row + n) * KT, :],
                              w[name].rearrange("a (k p) -> (a k) p", p=P)).then_inc(tables_landed, 16)
            for ln in range(NORMS):
                for j, vec in enumerate(norm_vectors(ln)):
                    row = 5 + 2 * ln + j
                    sp.dma_start(chan_rows[row * KT:(row + 1) * KT, :],
                                  vec.rearrange("a (k p) -> (a k) p", p=P)).then_inc(tables_landed, 16)
            sp.dma_start(sink[:], w["attn_sink"][0:1, :].to_broadcast([P, NH])).then_inc(tables_landed, 16)
            for p in range(RAW, 8):
                column_piece(B_PW1 + p, w["conv_w_pw1"][0], (p // 2 % 2) * D + (p // 4) * P, p % 2)
            with sp.Fori(1, KT // 2) as i:
                for p in range(8):
                    c, j = p // 4, p % 4
                    sp.wait_ge(piece_split, i * 8 + p - RAW + 1)
                    view = w["conv_w_pw1"][0].rearrange("(k p) f -> p k f", p=P)
                    sp.dma_start(raw[:, p % RAW, :].rearrange("p (k f) -> p k f", f=P),
                                 view[:, 4 * (j % 2):4 * (j % 2) + 4,
                                      bass.ds(i * 2 * P + (j // 2) * D + c * P, P)]
                                 ).then_inc(raw_landed[p % RAW], 16)
            for n in range(2):
                for k in range(KT):
                    row_piece(B_PW2 + n * KT + k, w["conv_w_pw2"][0, cols(k), n * HALF:(n + 1) * HALF])

            def ffn_pieces(layer):
                up, down, base = w["ffn_w_up"][layer], w["ffn_w_down"][layer], FFN_BASE[layer]
                with sp.Fori(0, GROUPS // 2) as i:
                    for g in range(2):
                        for j in range(8):
                            f = 2 * g + j // 4
                            column_piece(base + 12 * g + j, up, i * 4 * P + f * P + (j // 2 % 2) * F,
                                         j % 2, earlier=i * 24)
                        for j in range(4):
                            row_piece(base + 12 * g + 8 + j,
                                      down[bass.ds(i * 4 * P + (2 * g + j % 2) * P, P),
                                           (j // 2) * HALF:(j // 2 + 1) * HALF], earlier=i * 24)
                p = base + 12 * GROUPS
                for j in range(4):
                    column_piece(p + j, up, (FT - 1) * P + (j // 2) * F, j % 2)
                rest = up.rearrange("(k p) (s f) -> p k s f", p=P, s=2)[:, :, :, FT * P:F]
                for half in range(2):
                    paired_piece(p + 4 + half, rest, half)
                for j in range(4):
                    n = j // 2
                    if j % 2 == 0:
                        row_piece(p + 6 + j, down[(FT - 1) * P:FT * P, n * HALF:(n + 1) * HALF])
                    else:
                        row_piece(p + 6 + j, down[FT * P:F, n * HALF:(n + 1) * HALF], height=FR)

            ffn_pieces(0)
            for j in range(4):
                column_piece(B_KV + j, w["attn_w_kv"][0], (j // 2) * P, j % 2)
            for j in range(4):
                column_piece(B_KV + 4 + j, w["attn_w_kv"][0], KVD, j, n=2, width=KVD)
            q_cols = w["attn_w_q"][0].rearrange("(k p) (rr s r d) -> p k rr s r d", p=P, rr=2, s=2, r=GROUP)
            for c in range(KT):
                for half in range(2):
                    paired_piece(B_Q + 2 * c + half, q_cols[:, :, c // GROUP, :, c % GROUP, :], half)
            o_rows = w["attn_w_o"][0].rearrange("(rr s r d) n -> rr s r d n", rr=2, s=2, r=GROUP)
            for n in range(2):
                for k in range(KT):
                    p = B_O + n * KT + k
                    slot_free(p)
                    for s in range(2):
                        sp.dma_start(raw[s * HD:(s + 1) * HD, p % RAW, :],
                                     o_rows[k // GROUP, s, k % GROUP, :, n * HALF:(n + 1) * HALF]
                                     ).then_inc(raw_landed[p % RAW], 16)
            ffn_pieces(1)
            for t in range(TT):
                sp.wait_ge(out_ready, t + 1)
                sp.dma_start(out_rows[t], y[:, t, :]).then_inc(out_stored, 16)
            sp.wait_ge(out_stored, 16 * TT)

        ATT = [(n, rr, par) for n in range(TT) for rr in range(2) for par in range(2)]

        def key_blocks(n):
            lo, hi = (0, T0) if n < T0 else (T0, TT)
            return range(max(lo, n - 1), min(hi, n + 2))

        KEYS_TO = [sum(len(key_blocks(n)) for n, _, _ in ATT[:i]) for i in range(len(ATT) + 1)]
        SCORE_BANKS = (0, 1, 7)

        N_TABLE_DMAS = 8 * DEPTH + 6 + 2 * NORMS
        V_TAPS = TAPS - PE_TAPS

        EARLY = 4

        def more_diag(j):
            where = slice(None), j // TT, cols(j % TT)
            return XH[where], XL[where]

        FT_ALL = FT + 1
        N_DOWN = 20 * (GROUPS + 1)
        N_PROJ = 2 * TT
        GAINS_BY = [32, 64, 96, 128]
        TURN_BANK = [[4, 6, 4, 6, 4, 6, 4, 6, 4, 4], [0, 2, 2, 4, 6] + [4, 6, 4, 6, 4], [0] * TT,
                     [0, 2, 2, 4, 6] + [4, 6, 4, 6, 4]]
        RES_SPLIT = TT // 2

        def RES_DONE(r, t):
            if r != 1 and t >= RES_SPLIT:
                return residual_pool, (TT - RES_SPLIT) * (r // 2) + t - RES_SPLIT + 1
            return residual_done, [0, RES_SPLIT, RES_SPLIT + TT][r] + t + 1

        SCALED_TILE = [scaled_tile, scaled_end, scaled_tile]
        TILES_TO = [(c0 + n) // P for c0, n in CHUNKS]
        GLU_COL = [PAD, PAD + HALF, PAD + S0 + PAD]
        H_CHUNK = [0 if (t + 1) * P < HALF else 1 if t < T0 else 2 for t in range(TT)]
        CONV_CHUNKS = [(0, HALF - 1, 0), (HALF - 1, HALF + 1, HALF - 1), (S0, S1, S0 + 1)]
        RAW_COL = [1, 1 + HALF, 1 + S0 + 1]

        def ffn_before(layer):
            return 3 * FT_ALL * layer, N_DOWN * layer

        def bank_before(m):
            same = [b for b in range(m) if b % TT % 8 == m % TT % 8]
            return same[-1] if same else None

        BLOCKS = [(0, 4), (4, 8), (8, TT)]
        H_TILE = [min(t * P // HALF, 2) for t in range(TT)]

        def steps(text):
            out = []
            for item in text.split(","):
                what, j = item.split()
                out.append((what, tuple(int(v) for v in j.split(".")) if "." in j else int(j)))
            return out

        END_ORDER = steps("down 0, down 1, down 2, down 3, down 4, down 5, turn 0, turn 1, turn 2, "
                          "turn 3, down 6, down 7, k 0.0, turn 4, turn 5, down 8, down 9, k 1.0, turn 6, "
                          "turn 7, v 0, v 1, turn 8, v 2, v 3, turn 9, k 0.1, k 1.1, v 4, v 5, v 6, v 7, "
                          "k 0.2, k 1.2, v 8, v 9")
        END_ORDER_V = steps("add 0, add 1, add 2, add 3, stats 0, stats 1, norm 0, stats 2, norm 1, stats 3, "
                            "norm 2, add 4, add 5, norm 3, split 0, stats 4, split 1, stats 5, norm 4, split 2, "
                            "norm 5, split 3, add 6, add 7, stats 6, stats 7, norm 6, split 4, norm 7, split 5, "
                            "add 8, add 9, stats 8, stats 9, norm 8, split 6, norm 9, split 7, split 8, split 9")
        END_ORDER_S = steps("dev 0, dev 1, dev 2, dev 3, gain 0, gain 1, dev 4, gain 2, dev 5, gain 3, dev 6, "
                            "dev 7, k 0.0, gain 4, gain 5, dev 8, dev 9, k 1.0, gain 6, gain 7, v 0, v 1, "
                            "gain 8, v 2, v 3, gain 9, k 0.1, k 1.1, v 4, v 5, v 6, v 7, k 0.2, k 1.2, v 8, v 9")
        PROJ_ORDER_V = steps("add 0, add 1, add 2, add 3, stats 0, stats 1, norm 0, stats 2, norm 1, stats 3, "
                             "norm 2, norm 3, add 4, add 5, add 6, add 7, split 0, stats 4, split 1, stats 5, "
                             "split 2, norm 4, add 8, add 9, split 3, norm 5, stats 6, stats 7, norm 6, norm 7, "
                             "stats 8, split 4, stats 9, split 5, norm 8, norm 9, split 6, split 7, split 8, split 9")
        PROJ_ORDER_S = steps("dev 0, dev 1, dev 2, dev 3, gain 0, gain 1, dev 4, dev 5, gain 2, gain 3, dev 6, "
                             "dev 7, gain 4, dev 8, gain 5, dev 9, gain 6, gain 7, gain 8, gain 9")

        @block.gpsimd
        def _(pool):
            step = Count()
            pool.memset(ident[:], 0.0).then_inc(pool_step, step.one())
            pool.wait_ge(pool_step, step.now())
            pool.affine_select(out=ident[:], in_=ident[:], compare_op=ALU.not_equal, fill=1.0, base=0,
                               pattern=[[-1, P]], channel_multiplier=1).then_inc(consts_ready, 1)
            pool.memset(eps[:], EPS).then_inc(consts_ready, 1)

            def split(p, landed_value, used_value):
                pool.wait_ge(raw_landed[p % RAW], landed_value)
                if used_value is not None:
                    pool.wait_ge(piece_used, used_value)
                pool.sem_inc(pool_passed, 1)
                pool.tensor_copy(WH[:, p % RING, :], raw[:, p % RAW, :]).then_inc(piece_hi, 1)

            def split_low(p, hi_value):
                pool.wait_ge(piece_hi, hi_value)
                pool.tensor_tensor(WL[:, p % RING, :], raw[:, p % RAW, :], WH[:, p % RING, :].bitcast(F32),
                                   ALU.subtract).then_inc(piece_split, 1)

            pool.iota(dist_i[:], pattern=[[-1, 3 * P]], base=P, channel_multiplier=1).then_inc(pool_step, step.one())
            pool.wait_ge(pool_step, step.now())
            pool.tensor_copy(dist[:], dist_i[:]).then_inc(pool_step, step.one())
            pool.wait_ge(pool_step, step.now())
            pool.affine_select(out=dist[:], in_=dist[:], compare_op=ALU.is_ge, fill=FAR, base=0,
                               pattern=[[1, 3 * P]], channel_multiplier=-1).then_inc(pool_step, step.one())
            pool.wait_ge(pool_step, step.now())
            pool.affine_select(out=dist[:], in_=dist[:], compare_op=ALU.is_ge, fill=FAR, base=2 * P,
                               pattern=[[-1, 3 * P]], channel_multiplier=1).then_inc(consts_ready, 1)

            for p in range(RING):
                split(p, landed(p), None)
                split_low(p, p + 1)
            def stretch(first, end):
                rounds = (end - first) // RING
                per = 16 * (RING // RAW) * transfers[first]
                if rounds > 1:
                    with pool.Fori(0, rounds) as i:
                        for p in range(first, first + RING):
                            split(p, i * per + landed(p), i * RING + p - RING + 1)
                            split_low(p, i * RING + p + 1)
                    first += rounds * RING
                for p in range(first, end):
                    split(p, landed(p), p - RING + 1)
                    split_low(p, p + 1)

            def normalise_half(i):
                nk, b = len(key_blocks(ATT[i][0])) * P, i % 3
                pool.wait_ge(recip_ready, i + 1)
                for r in range(GROUP // 2, GROUP):
                    ins = pool.tensor_scalar(probs[:, b, r, 0:nk], probs[:, b, r, 0:nk], srec[:, b, r:r + 1],
                                             None, ALU.mult)
                ins.then_inc(probs_ready_pool, 1)

            def pool_residual(r):
                pool.wait_ge(gains_ready, r + 1)
                pool.wait_ge(turned_lo, 2 * TT * (r + 2))
                for t in range(RES_SPLIT, TT):
                    pool.tensor_tensor(y[:, t, :], y[:, t, :], gain[:], ALU.mult).then_inc(pool_step, step.one())
                    pool.wait_ge(pool_step, step.now())
                    pool.tensor_tensor(y[:, t, :], y[:, t, :], shift[:], ALU.add).then_inc(residual_pool, 1)

            rest0, rest1 = (b + 12 * GROUPS + 4 for b in FFN_BASE)
            stretch(RING, B_FFN0 + 12)
            pool_residual(0)
            stretch(B_FFN0 + 12, rest0)
            stretch(rest0, rest0 + 2)
            stretch(rest0 + 2, B_Q)
            stretch(B_Q, B_O)
            for i in range(len(ATT)):
                if i < RING - 1:
                    stretch(B_O + i, B_O + i + 1)
                normalise_half(i)
            stretch(B_O + RING - 1, B_FFN1)
            stretch(B_FFN1, B_FFN1 + 12)
            pool_residual(2)
            stretch(B_FFN1 + 12, rest1)
            stretch(rest1, rest1 + 2)
            stretch(rest1 + 2, N_PIECES)
            pool.wait_ge(gains_landed, GAINS_BY[3])
            for t in range(TT):
                pool.wait_ge(out_normed, t + 1)
                pool.tensor_tensor(y[:, t, :], y[:, t, :], shift[:], ALU.add).then_inc(out_ready, 1)

        @block.tensor
        def _(pe):
            owed = [False]

            def product(out, left, right, first, last, uses=0):
                mm = pe.matmul(out, left[0], right[0], start=first, stop=False)
                if owed[0]:
                    mm.then_inc(piece_used, 1)
                pe.matmul(out, left[0], right[1], start=False, stop=False)
                owed[0] = bool(uses)
                return pe.matmul(out, left[1], right[0], start=False, stop=last)

            def rounds(count, body):
                body(0, True)
                with pe.Fori(1, count) as i:
                    body(i, False)

            def wblock(p, k):
                s = (p + k // 4) % RING
                c = slice((k % 4) * P, (k % 4 + 1) * P)
                return WH[:, s, c], WL[:, s, c]

            def xpart(k, c0, n):
                return XH[:, k, c0:c0 + n], XL[:, k, c0:c0 + n]

            def turn_tile(use, t):
                before = [s for s in range(t) if TURN_BANK[use][s] == TURN_BANK[use][t]]
                if use > 0:
                    pe.wait_ge(ln_ready, TT * (use - 1) + t + 1)
                    if before:
                        pe.wait_ge(gained, TT * (use - 1) + before[-1] + 1)
                for half in range(2):
                    if use == 0 and before:
                        pe.wait_ge(turned_lo, 2 * before[-1] + half + 1)
                    for j in range(4):
                        mm = pe.transpose(bank[TURN_BANK[use][t] + half][:, cols(j)],
                                          y[:, t, cols(4 * half + j)], ident[:])
                    mm.then_inc(turned, 1)

            def turn_x(t):
                pe.wait_ge(x_landed[t], 16)
                turn_tile(0, t)

            pe.wait_ge(consts_ready, 2)
            for t in range(TILES_TO[0]):
                turn_x(t)
            def turn_tables():
                pe.wait_ge(consts_ready, 3)
                pe.wait_ge(tables_landed, 16 * N_TABLE_DMAS)
                pe.wait_ge(turned_lo, 2 * TILES_TO[1])
                for layer in range(DEPTH):
                    for tap in range(4):
                        o = (4 * layer + tap) * CONV_COLS
                        mm = pe.transpose(bank[6][:, o:o + CONV_COLS], ffn_rows[:, layer, tap, :],
                                          ident[0:CONV_COLS, 0:CONV_COLS])
                mm.then_inc(tab_turned, 1)
                for k in range(KT):
                    mm = pe.transpose(bank[7][:, k * TAPS:(k + 1) * TAPS], conv_rows[:, cols(k)],
                                      ident[0:TAPS, 0:TAPS])
                mm.then_inc(tab_turned, 1)
                n = (5 + 2 * NORMS) * KT
                pe.transpose(bank[7][:, KT * TAPS:KT * TAPS + n], chan_rows[:, :], ident[0:n, 0:n]
                             ).then_inc(tab_turned, 1)

            def back_tile(t):
                pe.wait_ge(cn_ready, t + 1)
                if t >= 2:
                    pe.wait_ge(silu_ready, t - 1)
                for k in range(KT):
                    mm = pe.transpose(bank[4 + 2 * (t % 2) + k // 4][:, cols(k % 4)], normed[:, t, cols(k)],
                                      ident[:])
                mm.then_inc(cn_turned, 1)

            def pair_chunk(p, left, right, c0, n, last_chunk, between={}):
                for b, q in ((left, p), (right, p + UNIT)):
                    for k in range(KT):
                        between.get(KT * (q > p) + k, lambda: None)()
                        mm = product(bank[b][:, 0:n], wblock(q, k), xpart(k, c0, n),
                                     k == 0, k == KT - 1, uses=last_chunk and k % 4 == 3)
                return mm

            def conv_taps(c, i, first, more=0):
                pe.wait_ge(diag_ready, i * 2 + c + (2 if more else 1))
                pe.wait_ge(glu_lo_ready, i * 2 + c + 1)
                for ch, (c0, n) in enumerate(CHUNKS):
                    u = 3 * c + ch
                    if not first or u >= 2:
                        pe.wait_ge(acc_ready, i * 6 + u - 1)
                    for j in range(-more, PE_TAPS):
                        at = GLU_COL[ch] - PAD + V_TAPS + j
                        left = (diag[:, 0, j, :], diag[:, 1, j, :]) if j >= 0 else more_diag(more + j)
                        mm = product(bank[6 + u % 2][:, 0:n], left, (glu_hi[:, at:at + n], glu_lo[:, at:at + n]),
                                     j == -more, j == PE_TAPS - 1)
                    mm.then_inc(taps_done, 1)

            def pw1_round(i, first):
                for c in range(2):
                    for ch, (c0, n) in enumerate(CHUNKS):
                        s = 3 * c + ch
                        if first and c == 0:
                            pe.wait_ge(turned_lo, 2 * TILES_TO[ch])
                        if ch == 0:
                            pe.wait_ge(piece_split, i * 8 + 4 * c + 4)
                        if not first or s >= 3:
                            pe.wait_ge(glu_done, i * 6 + s - 2)
                        turns = [range(TILES_TO[0], TILES_TO[1]), range(TILES_TO[1], TT)]
                        between = {}
                        if first and c == 0 and ch < 2:
                            between = {4 * (t % 4) + 2: (lambda t=t: turn_x(t)) for t in turns[ch]}
                            if ch == 1:
                                between[12] = turn_tables
                        pair_chunk(B_PW1 + 4 * c, 2 * ch, 2 * ch + 1, c0, n, ch == 2, between
                                   ).then_inc(pw1_done, 1)
                    if c == 1:
                        conv_taps(0, i, first)
                    elif not first:
                        conv_taps(1, i - 1, False)

            rounds(KT // 2, pw1_round)
            conv_taps(1, KT // 2 - 1, False, more=MORE_TAPS)

            pe.wait_ge(conv_done, KT)
            for t in range(TT):
                if t >= 2:
                    pe.wait_ge(ct_kept, t - 1)
                for k in range(KT):
                    mm = pe.transpose(bank[2 * (t % 2) + k // 4][:, cols(k % 4)], conv[:, k, cols(t)], ident[:])
                mm.then_inc(ct_turned, 1)

            def out_projection(base, use, between=None):
                norm = 2 * use
                turns = {(4, 4): 0, (4, 6): 1, (8, 0): 2, (8, 4): 3}
                for n in range(2):
                    for t0, t1 in BLOCKS:
                        for k in range(KT):
                            p = base + n * KT + k
                            pe.wait_ge(piece_split, p + 1)
                            for t in range(t0, t1):
                                before = bank_before(n * TT + t)
                                if k == 0 and before is not None:
                                    pe.wait_ge(proj_kept, N_PROJ * use + before + 1)
                                if k == 0 and n == 1 and t == 8:
                                    pe.wait_ge(gained, TT * norm + 1)
                                mm = product(bank[t % 8][:, :], xpart(k, t * P, P),
                                             (WH[:, p % RING, :], WL[:, p % RING, :]),
                                             k == 0, k == KT - 1, uses=(t == TT - 1))
                                if k == KT - 1:
                                    mm.then_inc(proj_done, 1)
                            if between and n == 0 and t0 == 0:
                                between(k)
                            if n == 1 and (t0, k) in turns:
                                if turns[t0, k] == 3:
                                    pe.wait_ge(proj_kept, N_PROJ * use + TT + 6)
                                turn_tile(norm + 1, turns[t0, k])
                        if between and n == 0 and t0 == 0:
                            pe.wait_ge(silu_lo, TT)

            for t in range(BLOCKS[0][1]):
                back_tile(t)
            pe.wait_ge(silu_lo, BLOCKS[0][1])
            out_projection(B_PW2, 0, lambda k: back_tile(BLOCKS[0][1] + k) if BLOCKS[0][1] + k < TT else None)

            def ffn(layer, use):
                base = FFN_BASE[layer]
                f0, d0 = ffn_before(layer)

                later = [{1: 4, 5: 5, 9: 6, 13: 7}, {2: 8, 4: 9}]

                def turns_between(s):
                    return {step: (lambda t=t: turn_tile(use, t)) for step, t in later[s].items()}

                def up_tile(p, i, s0, first):
                    for ch, (c0, n) in enumerate(CHUNKS):
                        s = s0 + ch
                        if first and s == 0:
                            pe.wait_ge(proj_kept, N_PROJ * (layer + 1))
                        if first and s < 3:
                            pe.wait_ge(turned_lo, 2 * (TT * use + TILES_TO[ch]))
                        if ch == 0:
                            pe.wait_ge(piece_split, i * 24 + p + 4)
                        if not first or s >= 2:
                            pe.wait_ge(ffn_raw, f0 + s - 1 + i * 12)
                        pair_chunk(p, 2 * (s % 2), 2 * (s % 2) + 1, c0, n, ch == 2,
                                   turns_between(s) if first and s < 2 else {}).then_inc(ffn_up, 1)

                def down_bank(p, i, m, t, n, h0, rows, first):
                    if n == 0:
                        pe.wait_ge(ffn_h, f0 + h0 + H_CHUNK[t] + 1 + i * 12)
                    if not first or m >= 4:
                        pe.wait_ge(down_kept, d0 + m - 3 + i * 40)
                    for j in range(2):
                        q = p + 2 * n + j
                        r = rows[j]
                        mm = product(bank[4 + m % 4][:, :], (HH[0:r, j, cols(t)], HL[0:r, j, cols(t)]),
                                     (WH[0:r, q % RING, :], WL[0:r, q % RING, :]),
                                     j == 0, j == 1, uses=(t == TT - 1))
                    mm.then_inc(down_done, 1)

                def two_groups(i, first):
                    for g in range(2):
                        p = base + 12 * g
                        for f in range(2):
                            up_tile(p + 4 * f, i, 6 * g + 3 * f, first)
                        for n in range(2):
                            pe.wait_ge(piece_split, i * 24 + p + 8 + 2 * n + 2)
                            for t in range(TT):
                                down_bank(p + 8, i, 20 * g + TT * n + t, t, n, 6 * g + 3, (P, P), first)

                rounds(GROUPS // 2, two_groups)
                p, s = base + 12 * GROUPS, 6 * GROUPS
                up_tile(p, 0, s, False)
                pe.wait_ge(piece_split, p + 6)
                for ch, (c0, n) in enumerate(CHUNKS):
                    pe.wait_ge(ffn_raw, f0 + s + 3 + ch - 1)
                    b = 2 * ((s + 3 + ch) % 2)
                    for k in range(KT):
                        mm = product(bank[b][:, 0:n], wblock(p + 4, k), xpart(k, c0, n),
                                     k == 0, k == KT - 1, uses=(ch == 2 and k % 4 == 3))
                    mm.then_inc(ffn_up, 1)
                pe.wait_ge(piece_split, p + 10)
                def last_down(t):
                    for n in range(2):
                        down_bank(p + 6, 0, 20 * GROUPS + 2 * t + n, t, n, s + 3, (P, FR), False)

                return last_down

            unit = 0

            def take_bank():
                nonlocal unit
                if unit >= 2:
                    pe.wait_ge(qkv_kept, unit - 1)
                unit += 1
                return bank[2 + (unit - 1) % 2]

            def channel_projection(p, ch):
                c0, n = CHUNKS[ch]
                out = take_bank()
                pe.wait_ge(piece_split, p + 2)
                for k in range(KT):
                    mm = product(out[:, 0:n], wblock(p, k), xpart(k, c0, n),
                                 k == 0, k == KT - 1, uses=(ch == 2 and k % 4 == 3))
                mm.then_inc(qkv_done, 1)

            def v_projection(t):
                out = take_bank()
                pe.wait_ge(piece_split, B_KV + 8)
                for k in range(KT):
                    q, c = (B_KV + 4 + k // 2) % RING, slice((k % 2) * KVD, (k % 2 + 1) * KVD)
                    mm = product(out[:, 0:KVD], xpart(k, t * P, P), (WH[:, q, c], WL[:, q, c]),
                                 k == 0, k == KT - 1, uses=(t == TT - 1 and k % 2 == 1))
                mm.then_inc(qkv_done, 1)

            last_down = ffn(0, 1)
            split_to = 0
            for what, j in END_ORDER:
                if what == "down":
                    last_down(j)
                elif what == "turn":
                    turn_tile(2, j)
                else:
                    ch = j[1] if what == "k" else H_TILE[j]
                    if ch >= split_to:
                        pe.wait_ge(turned_lo, 2 * (TT * 2 + TILES_TO[ch]))
                        split_to = ch + 1
                    if what == "k":
                        channel_projection(B_KV + 2 * j[0], ch)
                    else:
                        v_projection(j)
            for c in range(KT):
                for ch in range(3):
                    channel_projection(B_Q + 2 * c, ch)

            def scores(i):
                n, rr, par = ATT[i]
                kb = key_blocks(n)
                half = slice(par * HD, (par + 1) * HD)
                for r in range(GROUP):
                    u = GROUP * i + r
                    if u >= 3:
                        pe.wait_ge(score_kept, u - 2)
                    pe.matmul(bank[SCORE_BANKS[u % 3]][:, 0:len(kb) * P], q_sb[half, GROUP * rr + r, cols(n)],
                              k_sb[half, rr, kb[0] * P:(kb[-1] + 1) * P], start=True, stop=True
                              ).then_inc(score_done, 1)

            pe.wait_ge(qkv_kept, unit)
            for i in range(3):
                scores(i)
            for i, (n, rr, par) in enumerate(ATT):
                kb = key_blocks(n)
                if i >= 1:
                    pe.wait_ge(probs_T_kept, KEYS_TO[i])
                pe.wait_ge(probs_ready, i + 1)
                pe.wait_ge(probs_ready_pool, i + 1)
                for j in range(len(kb)):
                    for r in range(GROUP):
                        mm = pe.transpose(bank[2 + j][:, cols(r)], probs[:, i % 3, r, cols(j)], ident[:])
                    mm.then_inc(probs_turned, 1)
                if i + 3 < len(ATT):
                    scores(i + 3)
                if i >= 2:
                    pe.wait_ge(av_lo, i - 1)
                g = 2 * rr + par
                for j, b in enumerate(kb):
                    pe.wait_ge(probs_T_kept, KEYS_TO[i] + j + 1)
                    pe.matmul(bank[5 + i % 2][0:HD, :], v_sb[:, b, g * HD:(g + 1) * HD],
                              probsT[:, (KEYS_TO[i] + j) % 2, :], start=(j == 0), stop=(j == len(kb) - 1)
                              ).then_inc(av_done, 1)

            pe.wait_ge(av_lo, len(ATT))
            out_projection(B_O, 1)
            last_down = ffn(1, 3)
            for t in range(TT):
                last_down(t)

        @block.scalar
        def _(act):
            def rounds(count, body):
                body(0, True)
                with act.Fori(1, count) as i:
                    body(i, False)

            for t in range(TT):
                act.dma_start(y[:, t, :], x_rows[t]).then_inc(x_landed[t], 16)

            def load_gains(ln):
                for rows, vec in zip((gain, shift), norm_vectors(ln)):
                    act.dma_start(rows[:], vec.to_broadcast([P, D])).then_inc(gains_landed, 16)

            def scale_gains(ln):
                act.wait_ge(gains_landed, GAINS_BY[ln])
                for rows in (gain, shift):
                    ins = act.activation(rows[:], rows[:], ACT.Copy, scale=ALPHA)
                ins.then_inc(gains_ready, 1)

            def deviation(ln, t):
                act.wait_ge(var_ready, TT * ln + t + 1)
                act.activation(std[:, t:t + 1], mv[:, t, 1:2], ACT.Sqrt, bias=eps[:, 0:1]).then_inc(std_ready, 1)

            def keep_tile(ln, t):
                for half in range(2):
                    act.wait_ge(turned, 2 * (TT * (ln + 1) + t) + half + 1)
                    if half == 0 and t >= 2:
                        act.wait_ge(turned_lo, 2 * (TT * (ln + 1) + t - 1))
                    for k in range(4 * half, 4 * half + 4):
                        ins = act.activation(SCALED_TILE[ln][t % 2][:, k, :],
                                             bank[TURN_BANK[ln + 1][t] + half][:, cols(k % 4)],
                                             ACT.Identity, scale=chan[:, 5 + 2 * ln, k:k + 1],
                                             bias=chan[:, 6 + 2 * ln, k:k + 1])
                ins.then_inc(gained, 1)

            def norm_after_projection(ln):
                for what, t in PROJ_ORDER_S:
                    {"dev": deviation, "gain": keep_tile}[what](ln, t)

            def x_high(t):
                for half in range(2):
                    act.wait_ge(turned, 2 * t + half + 1)
                    act.activation(XH[:, 4 * half:4 * half + 4, cols(t)],
                                   bank[TURN_BANK[0][t] + half][:].rearrange("p (k t) -> p k t", t=P), ACT.Copy
                                   ).then_inc(turned_hi, 1)

            for t in range(TT):
                x_high(t)

            act.wait_ge(tab_kept, 7)

            def diagonals(c, i):
                act.sem_inc(act_passed, 1)
                for part, table in enumerate((tap_hi[:].bitcast(F32), tap_lo[:])):
                    for j in range(PE_TAPS):
                        ins = act.activation(diag[:, part, j, :], ident[:], ACT.Copy,
                                             scale=table[:, bass.ds(i * 2 + c, 1), j])
                ins.then_inc(diag_ready, 1)

            def keep_taps(c, i, first):
                for ch, (c0, n) in enumerate(CHUNKS):
                    u = 3 * c + ch
                    act.wait_ge(taps_done, i * 6 + u + 1)
                    if ch == 0 and (c == 1 or not first):
                        act.wait_ge(conv_done, i * 2 + (1 if c == 1 else -1))
                    act.sem_inc(act_passed, 1)
                    a0 = GLU_COL[ch] - PAD
                    act.activation(acc[:, c, a0:a0 + n], bank[6 + u % 2][:, 0:n], ACT.Identity,
                                   bias=chan[:, 0, bass.ds(i * 2 + c, 1)]).then_inc(acc_ready, 1)

            def pw1_round(i, first):
                for c in range(2):
                    for ch, (c0, n) in enumerate(CHUNKS):
                        s = 3 * c + ch
                        act.wait_ge(pw1_done, i * 6 + s + 1)
                        act.sem_inc(act_passed, 1)
                        act.activation(conv[:, bass.ds(i * 2 + c, 1), c0:c0 + n], bank[2 * ch + 1][:, 0:n],
                                       ACT.Sigmoid, bias=chan[:, 4, bass.ds(i * 2 + c, 1)]
                                       ).then_inc(sig_ready, 1)
                    if c == 1:
                        keep_taps(0, i, first)
                    elif not first:
                        keep_taps(1, i - 1, False)
                    act.wait_ge(glu_done, i * 6 + 3 * c + 3)
                    act.activation(glu_hi[:], glu[:, c, :], ACT.Copy).then_inc(glu_hi_ready, 1)
                    diagonals(c, i)

            rounds(KT // 2, pw1_round)
            for part, table in enumerate((more_hi[:].bitcast(F32), more_lo[:])):
                for j in range(MORE_TAPS):
                    ins = act.activation(more_diag(j)[part], ident[:], ACT.Copy, scale=table[:, j:j + 1])
            ins.then_inc(diag_ready, 1)
            keep_taps(1, KT // 2 - 1, False)
            for t in range(TT):
                act.wait_ge(ct_turned, t + 1)
                for half in range(2):
                    ins = act.activation(normed[:, t, half * HALF:(half + 1) * HALF],
                                         bank[2 * (t % 2) + half][:], ACT.Copy)
                ins.then_inc(ct_kept, 1)
                if t in (EARLY + 1, TT - 1):
                    t0, t1 = (0, EARLY) if t == EARLY + 1 else (EARLY, TT)
                    act.wait_ge(conv_var, t1)
                    act.activation(std[:, t0:t1], mv[:, t0:t1, 1], ACT.Sqrt, bias=eps[:, 0:1]).then_inc(conv_std, 1)
            for t in range(TT):
                act.wait_ge(cn_turned, t + 1)
                if t >= 2:
                    act.wait_ge(silu_lo, t - 1)
                for k in range(KT):
                    ins = act.activation(act_out[:, t % 2, k, :], bank[4 + 2 * (t % 2) + k // 4][:, cols(k % 4)],
                                         ACT.Silu, bias=chan[:, 2, k:k + 1], scale=chan[:, 1, k:k + 1])
                ins.then_inc(silu_ready, 1)
                act.wait_ge(silu_ready, t + 1)
                act.activation(XH[:, :, cols(t)], act_out[:, t % 2, :, :], ACT.Copy).then_inc(silu_hi, 1)
            act.dma_start(pw2_bias[:], w["conv_b_pw2"][0:1, :].to_broadcast([P, D])).then_inc(bias_landed, 16)
            for t in range(TT):
                if t == TT - 2:
                    act.wait_ge(silu_lo, TT)
                act.dma_start(y[:, t, :], x_rows[t]).then_inc(res_landed[t], 16)
            load_gains(0)
            scale_gains(0)
            norm_after_projection(0)

            def ffn(layer, use):
                f0, _ = ffn_before(layer)
                def chunk(i, s, ch, first, narrow=False):
                    n, col = CHUNKS[ch][1], RAW_COL[ch]
                    act.wait_ge(ffn_up, f0 + s + 1 + i * 12)
                    if not first or s >= 3:
                        act.wait_ge(ffn_conv, f0 + s - (1 if ch == 0 else 2) + i * 12)
                    for part in range(1 if narrow else 2):
                        ins = act.activation(gu_raw[:, part, col:col + n], bank[2 * (s % 2) + part][:, 0:n],
                                             ACT.Copy)
                    ins.then_inc(ffn_raw, 1)
                    act.wait_ge(ffn_gc, f0 + s + 1 + i * 12)
                    n, rows = CONV_CHUNKS[ch][1], FR if narrow else P
                    act.activation(g_conv[0:rows, 0:n], g_conv[0:rows, 0:n], ACT.Silu).then_inc(ffn_silu, 1)

                def two_groups(i, first):
                    for s in range(12):
                        chunk(i, s, s % 3, first)

                rounds(GROUPS // 2, two_groups)
                if layer + 1 == DEPTH:
                    act.wait_ge(*RES_DONE(2, RES_SPLIT - 1))
                    act.wait_ge(*RES_DONE(2, TT - 1))
                    load_gains(use)
                for s in range(6 * GROUPS, 6 * GROUPS + 6):
                    chunk(0, s, s % 3, False, narrow=s >= 6 * GROUPS + 3)
                if layer + 1 == DEPTH:
                    for t in range(TT + 1):
                        if t < TT:
                            deviation(use, t)
                        if t >= 1:
                            act.wait_ge(out_gained, t)
                            act.wait_ge(inverse_ready, t)
                            act.activation(y[:, t - 1, :], y[:, t - 1, :], ACT.Copy, scale=rstd[:, t - 1:t]
                                           ).then_inc(out_normed, 1)

            ffn(0, 1)

            unit = 0

            def keep(out, n, scale=1.0):
                nonlocal unit
                act.wait_ge(qkv_done, unit + 1)
                act.activation(out, bank[2 + unit % 2][:, 0:n], ACT.Copy, scale=scale).then_inc(qkv_kept, 1)
                unit += 1

            for what, j in END_ORDER_S:
                if what == "dev":
                    deviation(1, j)
                elif what == "gain":
                    keep_tile(1, j)
                    act.dma_start(residual_rows[j], y[:, j, :]).then_inc(res_stored, 16)
                elif what == "k":
                    c0, n = CHUNKS[j[1]]
                    keep(k_sb[:, j[0], c0:c0 + n], n)
                else:
                    keep(v_sb[:, j, :], KVD)
            act.wait_ge(res_stored, 16 * TT)
            for c in range(KT):
                for c0, n in CHUNKS:
                    keep(q_sb[:, c, c0:c0 + n], n, scale=HD ** -0.5)

            def exponentials(i):
                n, rr, par = ATT[i]
                nk, b = len(key_blocks(n)) * P, i % 3
                act.wait_ge(max_ready, i + 1)
                for r in range(GROUP):
                    act.activation(probs[:, b, r, 0:nk], probs[:, b, r, 0:nk], ACT.Exp,
                                   bias=nmax[:, b, r:r + 1], accum_out=ssum[:, b, r:r + 1])
                act.activation(sexp[:, b, :], sexp[:, b, :], ACT.Exp).then_inc(exp_ready, 1)

            for i in range(3):
                exponentials(i)
            for i, (n, rr, par) in enumerate(ATT):
                for j in range(len(key_blocks(n))):
                    u = KEYS_TO[i] + j
                    act.wait_ge(probs_turned, u + 1)
                    if u >= 2:
                        act.wait_ge(av_done, u - 1)
                    act.activation(probsT[:, u % 2, :], bank[2 + j][:, :], ACT.Copy).then_inc(probs_T_kept, 1)
                act.wait_ge(av_done, KEYS_TO[i + 1])
                act.activation(XH[par * HD:(par + 1) * HD, GROUP * rr:GROUP * (rr + 1), cols(n)],
                               bank[5 + i % 2][0:HD, :].rearrange("p (k t) -> p k t", t=P), ACT.Copy
                               ).then_inc(av_hi, 1)
                if i + 3 < len(ATT):
                    exponentials(i + 3)
            act.wait_ge(av_lo, len(ATT))
            for t in range(TT):
                act.dma_start(y[:, t, :], residual_rows[t]).then_inc(res_landed[t], 16)
            act.wait_ge(*RES_DONE(0, TT - 1))
            load_gains(1)
            scale_gains(1)
            act.wait_ge(*RES_DONE(1, TT - 1))
            load_gains(2)
            scale_gains(2)
            norm_after_projection(2)
            ffn(1, 3)

        @block.vector
        def _(dve):
            vs = Count()

            def keep_split(use, t):
                whole = SCALED_TILE[use - 1][t % 2]
                dve.wait_ge(gained, TT * (use - 1) + t + 1)
                dve.tensor_copy(XH[:, :, cols(t)], whole[:]).then_inc(vec_step, vs.one())
                dve.wait_ge(vec_step, vs.now())
                dve.tensor_tensor(XL[:, :, cols(t)], whole[:], XH[:, :, cols(t)].bitcast(F32), ALU.subtract
                                  ).then_inc(turned_lo, 2)

            def norm_stats(ln, t, written):
                dve.wait_ge(*written)
                for half in range(2):
                    dve.bn_stats(stats[:, t % 2, half, :], y[:, t, half * HALF:(half + 1) * HALF]
                                 ).then_inc(vec_step, vs.one())
                dve.wait_ge(vec_step, vs.now())
                dve.bn_aggr(mv[:, t, :], stats[:, t % 2, :, :]).then_inc(var_ready, 1)

            def norm_apply(ln, t):
                dve.wait_ge(std_ready, TT * ln + t + 1)
                dve.reciprocal(rstd[:, t:t + 1], std[:, t:t + 1]).then_inc(vec_step, vs.one())
                dve.wait_ge(vec_step, vs.now())
                dve.wait_ge(var_ready, TT * ln + t + 1)
                dve.tensor_scalar(y[:, t, :], y[:, t, :], mv[:, t, 0:1], rstd[:, t:t + 1], ALU.subtract,
                                  ALU.mult).then_inc(ln_ready, 1)

            def residual_tile(r, t):
                dve.wait_ge(gains_ready, r + 1)
                dve.tensor_tensor(y[:, t, :], y[:, t, :], gain[:], ALU.mult).then_inc(res_step, 1)
                dve.wait_ge(res_step, RES_DONE(r, t)[1])
                dve.tensor_tensor(y[:, t, :], y[:, t, :], shift[:], ALU.add).then_inc(residual_done, 1)

            def x_low(t):
                for half in range(2):
                    k = slice(4 * half, 4 * half + 4)
                    dve.wait_ge(turned_hi, 2 * t + half + 1)
                    dve.tensor_tensor(XL[:, k, cols(t)],
                                      bank[TURN_BANK[0][t] + half][:].rearrange("p (k t) -> p k t", t=P),
                                      XH[:, k, cols(t)].bitcast(F32), ALU.subtract).then_inc(turned_lo, 1)
            for t in range(TT):
                x_low(t)
            dve.wait_ge(tab_turned, 1)
            dve.tensor_copy(ffn_tab[:].rearrange("p l t c -> p (l t c)"), bank[6][:, 0:4 * DEPTH * CONV_COLS]
                            ).then_inc(tab_kept, 1)
            dve.wait_ge(tab_turned, 3)
            dve.tensor_copy(conv_tab[:].rearrange("p k t -> p (k t)"), bank[7][:, 0:KT * TAPS]).then_inc(tab_kept, 1)
            dve.tensor_copy(chan[:].rearrange("p v k -> p (v k)"), bank[7][:, KT * TAPS:(TAPS + 5 + 2 * NORMS) * KT]
                            ).then_inc(tab_kept, 1)
            dve.wait_ge(tab_kept, 3)
            more = conv_tab[:, KT - 1, V_TAPS - MORE_TAPS:V_TAPS]
            dve.tensor_copy(tap_hi[:], conv_tab[:, :, V_TAPS:TAPS]).then_inc(tab_kept, 1)
            dve.tensor_copy(more_hi[:], more).then_inc(tab_kept, 1)
            dve.wait_ge(tab_kept, 5)
            dve.tensor_tensor(tap_lo[:], conv_tab[:, :, V_TAPS:TAPS], tap_hi[:].bitcast(F32), ALU.subtract
                              ).then_inc(tab_kept, 1)
            dve.tensor_tensor(more_lo[:], more, more_hi[:].bitcast(F32), ALU.subtract).then_inc(tab_kept, 1)
            dve.wait_ge(consts_ready, 3)
            dve.memset(glu[:], 0.0).then_inc(vec_step, vs.one())
            dve.memset(acc[:], 0.0).then_inc(vec_step, vs.one())
            dve.wait_ge(vec_step, vs.now())
            dve.wait_ge(tab_kept, 5)

            def glu_low(c, i):
                dve.wait_ge(glu_hi_ready, i * 2 + c + 1)
                dve.tensor_tensor(glu_lo[:], glu[:, c, :], glu_hi[:].bitcast(F32), ALU.subtract
                                  ).then_inc(glu_lo_ready, 1)

            def conv_taps(c, i, between=lambda: None, taps=V_TAPS):
                tap = lambda k: conv_tab[:, bass.ds(i * 2 + c, 1), k]
                dve.wait_ge(acc_ready, i * 6 + 3 * c + 3)
                for k in range(taps):
                    last = k == taps - 1
                    for c0, n, a0 in ((0, S0, 0), (S0, S1, S0 + PAD)):
                        if k > 0:
                            dve.wait_ge(vec_step, vs.now() - (0 if last and c0 else 1))
                        ins = dve.scalar_tensor_tensor(
                            out=conv[:, bass.ds(i * 2 + c, 1), c0:c0 + n] if last else acc[:, c, a0:a0 + n],
                            in0=glu[:, c, a0 + k:a0 + k + n], scalar=tap(k), in1=acc[:, c, a0:a0 + n],
                            op0=ALU.mult, op1=ALU.add)
                        if not last:
                            ins.then_inc(vec_step, vs.one())
                    if k == 3:
                        between()
                ins.then_inc(conv_done, 1)

            def conv_round(i, first):
                for c in range(2):
                    if not first:
                        dve.wait_ge(conv_done, i * 2 + c - 1)
                    for ch, (c0, n) in enumerate(CHUNKS):
                        s = 3 * c + ch
                        dve.wait_ge(sig_ready, i * 6 + s + 1)
                        dve.scalar_tensor_tensor(
                            out=glu[:, c, GLU_COL[ch]:GLU_COL[ch] + n], in0=bank[2 * ch][:, 0:n],
                            scalar=chan[:, 3, bass.ds(i * 2 + c, 1)],
                            in1=conv[:, bass.ds(i * 2 + c, 1), c0:c0 + n],
                            op0=ALU.add, op1=ALU.mult).then_inc(glu_done, 1)
                    if c == 1:
                        conv_taps(0, i, lambda: glu_low(1, i))
                    elif first:
                        glu_low(0, 0)
                    else:
                        conv_taps(1, i - 1, lambda: glu_low(0, i))

            vs.rounds(dve, KT // 2, conv_round, 2 * 2 * (V_TAPS - 1))
            conv_taps(1, KT // 2 - 1, taps=V_TAPS - MORE_TAPS)

            def conv_stats(t):
                dve.wait_ge(ct_kept, t + 1)
                for half in range(2):
                    dve.bn_stats(stats[:, t % 2, half, :], normed[:, t, half * HALF:(half + 1) * HALF]
                                 ).then_inc(vec_step, vs.one())
                dve.wait_ge(vec_step, vs.now())
                dve.bn_aggr(mv[:, t, :], stats[:, t % 2, :, :]).then_inc(conv_var, 1)

            def conv_deviations(part):
                t0, t1 = ((0, EARLY), (EARLY, TT))[part]
                dve.wait_ge(conv_std, part + 1)
                dve.reciprocal(rstd[:, t0:t1], std[:, t0:t1]).then_inc(vec_step, vs.one())
                dve.wait_ge(vec_step, vs.now())
                dve.wait_ge(conv_var, t1)

            def silu_low(t):
                dve.wait_ge(silu_hi, t + 1)
                dve.tensor_tensor(XL[:, :, cols(t)], act_out[:, t % 2, :, :], XH[:, :, cols(t)].bitcast(F32),
                                  ALU.subtract).then_inc(silu_lo, 1)

            def conv_norm(t):
                dve.tensor_scalar(normed[:, t, :], normed[:, t, :], mv[:, t, 0:1], rstd[:, t:t + 1],
                                  ALU.subtract, ALU.mult).then_inc(cn_ready, 1)

            for t in range(EARLY + 3):
                conv_stats(t)
            conv_deviations(0)
            for t in range(EARLY):
                conv_norm(t)
                if EARLY + 3 + t < TT:
                    conv_stats(EARLY + 3 + t)
            conv_deviations(1)
            for t in range(TT):
                if t + EARLY < TT:
                    conv_norm(t + EARLY)
                silu_low(t)

            def out_projection(use, ln):
                def add(n, t):
                    m, half = n * TT + t, slice(n * HALF, (n + 1) * HALF)
                    dve.wait_ge(proj_done, N_PROJ * use + m + 1)
                    dve.tensor_tensor(y[:, t, half], y[:, t, half], bank[t % 8][:], ALU.add
                                      ).then_inc(proj_kept, 1)

                for t in range(TT):
                    dve.wait_ge(res_landed[t], 16 * (use + 1))
                    if use:
                        residual_tile(1, t)
                        dve.wait_ge(*RES_DONE(1, t))
                    else:
                        dve.wait_ge(bias_landed, 16)
                        dve.scalar_tensor_tensor(out=y[:, t, :], in0=y[:, t, :], scalar=ALPHA,
                                                 in1=pw2_bias[:], op0=ALU.mult, op1=ALU.add
                                                 ).then_inc(vec_step, vs.one())
                        dve.wait_ge(vec_step, vs.now())
                    add(0, t)
                for what, t in PROJ_ORDER_V:
                    if what == "add":
                        add(1, t)
                    elif what == "stats":
                        norm_stats(ln, t, (proj_kept, N_PROJ * use + TT + t + 1))
                    elif what == "norm":
                        norm_apply(ln, t)
                    else:
                        keep_split(ln + 1, t)

            def ffn(layer, use):
                f0, d0 = ffn_before(layer)
                dve.wait_ge(turned_lo, 2 * TT * (use + 1))
                for col in (0, 1 + S0, 1 + S0 + 1 + S1):
                    dve.memset(gu_raw[:, :, col:col + 1], 0.0).then_inc(vec_step, vs.one())
                dve.wait_ge(vec_step, vs.now())

                def conv3(out, part, ch, col, last_sem, rows=P):
                    _, n, a0 = CONV_CHUNKS[ch]
                    tab = lambda tap: ffn_tab[:, layer, tap, col]
                    dve.tensor_scalar(out[:, 0:n], gu_raw[:, part, a0:a0 + n], tab(0), tab(3), ALU.mult,
                                      ALU.add).then_inc(vec_step, vs.one())
                    for tap in (1, 2):
                        dve.wait_ge(vec_step, vs.now())
                        ins = dve.scalar_tensor_tensor(
                            out=out[:, 0:n], in0=gu_raw[:, part, a0 + tap:a0 + tap + n], scalar=tab(tap),
                            in1=out[:, 0:n], op0=ALU.mult, op1=ALU.add)
                        if tap == 1:
                            ins.then_inc(vec_step, vs.one())
                    ins.then_inc(last_sem, 1)

                def split_hidden(i, s, ch, slot, rows):
                    c0, n, _ = CONV_CHUNKS[ch]
                    dve.wait_ge(ffn_silu, f0 + s + 1 + i * 12)
                    dve.wait_ge(ffn_conv, f0 + s + 1 + i * 12)
                    u, hi, lo = u_conv[0:rows, 0:n], HH[0:rows, slot, c0:c0 + n], HL[0:rows, slot, c0:c0 + n]
                    dve.tensor_tensor(u, g_conv[0:rows, 0:n], u, ALU.mult).then_inc(vec_step, vs.one())
                    dve.wait_ge(vec_step, vs.now())
                    dve.tensor_copy(hi, u).then_inc(vec_step, vs.one())
                    dve.wait_ge(vec_step, vs.now())
                    dve.tensor_tensor(lo, u, hi.bitcast(F32), ALU.subtract).then_inc(ffn_h, 1)
                    dve.wait_ge(ffn_h, f0 + s + 1 + i * 12)

                def chunk(i, s, ch, slot, f, group_done, between=lambda: None):
                    dve.wait_ge(ffn_raw, f0 + s + 1 + i * 12)
                    conv3(g_conv, 0, ch, bass.ds(i * 4 + f, 1), ffn_gc)
                    conv3(u_conv, 1, ch, bass.ds(i * 4 + FT + f, 1), ffn_conv)
                    between()
                    if group_done is not None:
                        dve.wait_ge(down_done, group_done)
                    split_hidden(i, s, ch, slot, P)

                def add_down(i, m, t, n):
                    dve.wait_ge(down_done, d0 + m + 1 + i * 40)
                    half = slice(n * HALF, (n + 1) * HALF)
                    dve.tensor_tensor(y[:, t, half], y[:, t, half], bank[4 + m % 4][:], ALU.add
                                      ).then_inc(down_kept, 1)

                def two_groups(i, first):
                    for g in range(2):
                        def first_adds():
                            for t in range(2):
                                add_down(i, 20 * g + t, t, 0)

                        for f in range(2):
                            for ch in range(3):
                                done = None if first and g == 0 else d0 + 20 * g + i * 40
                                if first and g == 0 and 3 * f + ch > 0:
                                    residual_tile(use - 1, 3 * f + ch - 1)
                                if first and g == 0 and 3 * f + ch == 5:
                                    dve.wait_ge(*RES_DONE(use - 1, 1))
                                chunk(i, 6 * g + 3 * f + ch, ch, f, 2 * g + f, done,
                                      first_adds if 3 * f + ch == 5 else lambda: None)
                        for n in range(2):
                            for t in range(2 if n == 0 else 0, TT):
                                if first and g == 0 and n == 0:
                                    dve.wait_ge(*RES_DONE(use - 1, t))
                                add_down(i, 20 * g + TT * n + t, t, n)

                vs.rounds(dve, GROUPS // 2, two_groups, 72)
                s = 6 * GROUPS
                for ch in range(3):
                    chunk(0, s + ch, ch, 0, FT - 1, d0 + 20 * GROUPS)
                for ch in range(3):
                    n = CONV_CHUNKS[ch][1]
                    dve.wait_ge(ffn_raw, f0 + s + 3 + ch + 1)
                    conv3(g_conv, 0, ch, slice(2 * FT, 2 * FT + 1), ffn_conv)
                    dve.wait_ge(ffn_conv, f0 + s + 3 + ch + 1)
                    dve.tensor_copy(u_conv[0:FR, 0:n], g_conv[FR:P, 0:n]).then_inc(ffn_gc, 1)
                    dve.wait_ge(ffn_gc, f0 + s + 3 + ch + 1)
                    split_hidden(0, s + 3 + ch, ch, 1, FR)
                def last_add(t):
                    for n in range(2):
                        add_down(0, 20 * GROUPS + 2 * t + n, t, n)

                if layer + 1 < DEPTH:
                    for what, t in END_ORDER_V:
                        if what == "add":
                            last_add(t)
                        elif what == "stats":
                            norm_stats(use, t, (down_kept, d0 + 20 * GROUPS + 2 * t + 2))
                        elif what == "norm":
                            norm_apply(use, t)
                        else:
                            keep_split(use + 1, t)
                else:
                    for t in range(TT + 1):
                        if t < TT:
                            last_add(t)
                            norm_stats(use, t, (down_kept, d0 + 20 * GROUPS + 2 * t + 2))
                            dve.wait_ge(gains_landed, GAINS_BY[use])
                            dve.wait_ge(var_ready, TT * use + t + 1)
                            dve.scalar_tensor_tensor(out=y[:, t, :], in0=y[:, t, :], scalar=mv[:, t, 0:1],
                                                     in1=gain[:], op0=ALU.subtract, op1=ALU.mult
                                                     ).then_inc(out_gained, 1)
                        if t >= 1:
                            dve.wait_ge(std_ready, TT * use + t)
                            dve.reciprocal(rstd[:, t - 1:t], std[:, t - 1:t]).then_inc(inverse_ready, 1)

            out_projection(0, 0)
            ffn(0, 1)

            dve.wait_ge(tables_landed, 16 * N_TABLE_DMAS)
            dve.wait_ge(consts_ready, 3)
            dve.scalar_tensor_tensor(out=dist[:], in0=dist[:], scalar=-1.0, in1=dist[:], op0=ALU.mult,
                                     op1=ALU.max).then_inc(vec_step, vs.one())
            dve.wait_ge(vec_step, vs.now())

            def biased_scores(i):
                n, rr, par = ATT[i]
                kb = key_blocks(n)
                nk, d0, b = len(kb) * P, (kb[0] - n + 1) * P, i % 3
                h0 = GROUP * (2 * rr + par)
                if i >= 3:
                    dve.wait_ge(probs_turned, KEYS_TO[i - 2])
                for r in range(GROUP):
                    u = GROUP * i + r
                    dve.wait_ge(score_done, u + 1)
                    dve.scalar_tensor_tensor(out=probs[:, b, r, 0:nk], in0=dist[:, d0:d0 + nk],
                                             scalar=-SLOPES[h0 + r], in1=bank[SCORE_BANKS[u % 3]][:, 0:nk],
                                             op0=ALU.mult, op1=ALU.add).then_inc(score_kept, 1)
                dve.wait_ge(score_kept, GROUP * (i + 1))
                dve.tensor_reduce(nmax[:, b, :], probs[:, b, :, 0:nk], AX_X, ALU.max).then_inc(vec_step, vs.one())
                dve.wait_ge(vec_step, vs.now())
                dve.tensor_tensor(nmax[:, b, :], nmax[:, b, :], sink[:, h0:h0 + GROUP], ALU.max
                                  ).then_inc(vec_step, vs.one())
                dve.wait_ge(vec_step, vs.now())
                dve.tensor_scalar(nmax[:, b, :], nmax[:, b, :], -1.0, None, ALU.mult).then_inc(vec_step, vs.one())
                dve.wait_ge(vec_step, vs.now())
                dve.tensor_tensor(sexp[:, b, :], nmax[:, b, :], sink[:, h0:h0 + GROUP], ALU.add
                                  ).then_inc(max_ready, 1)

            def normalise(i):
                n, rr, par = ATT[i]
                nk, b = len(key_blocks(n)) * P, i % 3
                dve.wait_ge(exp_ready, i + 1)
                if i >= 3:
                    dve.wait_ge(probs_ready_pool, i - 2)
                dve.tensor_tensor(ssum[:, b, :], ssum[:, b, :], sexp[:, b, :], ALU.add).then_inc(vec_step, vs.one())
                dve.wait_ge(vec_step, vs.now())
                dve.reciprocal(srec[:, b, :], ssum[:, b, :]).then_inc(recip_ready, 1)
                dve.wait_ge(recip_ready, i + 1)
                for r in range(GROUP // 2):
                    ins = dve.tensor_scalar(probs[:, b, r, 0:nk], probs[:, b, r, 0:nk], srec[:, b, r:r + 1],
                                            None, ALU.mult)
                ins.then_inc(probs_ready, 1)

            def heads_low(i):
                n, rr, par = ATT[i]
                dve.wait_ge(av_hi, i + 1)
                where = slice(par * HD, (par + 1) * HD), slice(GROUP * rr, GROUP * (rr + 1)), cols(n)
                dve.tensor_tensor(XL[where], bank[5 + i % 2][0:HD, :].rearrange("p (k t) -> p k t", t=P),
                                  XH[where].bitcast(F32), ALU.subtract).then_inc(av_lo, 1)

            for i in range(3):
                biased_scores(i)
            normalise(0)
            for i in range(len(ATT)):
                if i + 1 < len(ATT):
                    normalise(i + 1)
                if i + 3 < len(ATT):
                    biased_scores(i + 3)
                if i >= 1:
                    heads_low(i - 1)
            heads_low(len(ATT) - 1)
            out_projection(1, 2)
            ffn(1, 3)


_INS = ["x_prompt", "x_sample", "conv_w_pw1", "conv_b_pw1", "conv_w_dw", "conv_b_dw", "conv_norm_g",
        "conv_norm_b", "conv_w_pw2", "conv_b_pw2", "attn_w_q", "attn_w_kv", "attn_w_o", "attn_sink",
        "ffn_w_up", "ffn_w_dw", "ffn_b_dw", "ffn_w_down", "ln_mix_g", "ln_mix_b", "ln_ffn_g", "ln_ffn_b"]


def kernel(**inputs):
    import numpy as _np
    import concourse.bacc as _bacc
    from concourse import mybir as _mybir
    from concourse.bass_utils import run_bass_kernel_spmd as _run

    nc = _bacc.Bacc("TRN2", target_bir_lowering=False, num_devices=1)
    arrays, weights = {}, {}
    for name in _INS:
        a = _np.ascontiguousarray(inputs[name])
        arrays[f"in_{name}_dram"] = a
        weights[name] = nc.dram_tensor(f"in_{name}_dram", a.shape, _mybir.dt.from_np(a.dtype),
                                       kind="ExternalInput").ap()
    f32 = _mybir.dt.float32
    prompt, sample = inputs["x_prompt"].shape, inputs["x_sample"].shape
    out0 = nc.dram_tensor("out_0_dram", prompt, f32, kind="ExternalOutput").ap()
    out1 = nc.dram_tensor("out_1_dram", sample, f32, kind="ExternalOutput").ap()
    residual = nc.dram_tensor("residual_dram", (prompt[1] + sample[1], prompt[2]), f32, kind="Internal").ap()
    trunk(nc, weights, out0, out1, residual)
    r = _run(nc, [arrays], core_ids=[0])
    return r.results[0]["out_0_dram"], r.results[0]["out_1_dram"]
```
